# Optimizing a Trainium2 kernel written in Bass

```python
import math
import jax, jax.numpy as jnp
from jax import lax
import numpy as np

D_MODEL = 1024
BATCH = 1
SEQ = 256
DEPTH = 2

HEAD_DIM = 64
A_HEADS = D_MODEL // 256
A_VDIM = 2 * HEAD_DIM
A_QK_WIDTH = A_HEADS * 2 * HEAD_DIM
A_V_WIDTH = A_HEADS * A_VDIM
B_HEADS = D_MODEL // 128
B_WIDTH = B_HEADS * HEAD_DIM
IN_WIDTH = 2 * A_QK_WIDTH + A_V_WIDTH + 3 * B_WIDTH
MIX_WIDTH = A_V_WIDTH + B_WIDTH
D_FF = 2816
GRID_W = 64
NA_ROWS = 8
NA_COLS = 16
POOL_WINDOWS = (2, 4, 8, 16)
POOL_GROUPS = 4
POOL_GROUP_DIM = D_MODEL // POOL_GROUPS
ROPE_THETA = 10000.0
Q_BLOCK = 128
EPS = 1e-6
N_MOD = 9
N_EVEN = (DEPTH + 1) // 2
N_ODD = DEPTH // 2
NEG_INF = -1e30

kernel_name = "hybrid_diffattn_natten_pool_macaron_adaln"

def rmsnorm(x, g):
    xf = x.astype(jnp.float32)
    y = xf * lax.rsqrt(jnp.mean(xf * xf, axis=-1, keepdims=True) + EPS)
    return (y * g.astype(jnp.float32)).astype(x.dtype)

def modulate(h, shift, scale):
    return h * (1 + scale[:, None, :]) + shift[:, None, :]

def swiglu(h, w13, w2):
    a, b = jnp.split(h @ w13, 2, axis=-1)
    return (jax.nn.silu(a) * b) @ w2

def rope(x, pos):
    d = x.shape[-1]
    inv = ROPE_THETA ** (-jnp.arange(0, d, 2, dtype=jnp.float32) / d)
    ang = pos.astype(jnp.float32)[:, None] * inv[None, :]
    cos = jnp.cos(ang).astype(x.dtype)
    sin = jnp.sin(ang).astype(x.dtype)
    x1, x2 = x[..., : d // 2], x[..., d // 2:]
    return jnp.concatenate([x1 * cos - x2 * sin, x1 * sin + x2 * cos], axis=-1)

def diff_attention(q, k, v, qk_norm, lam_params, subln_g, lambda_init):
    B_, S, H, _, d = q.shape
    pos = jnp.arange(S)
    q = rope(rmsnorm(q, qk_norm[0]).transpose(0, 2, 3, 1, 4), pos)
    k = rope(rmsnorm(k, qk_norm[1]).transpose(0, 2, 3, 1, 4), pos)
    v = v.transpose(0, 2, 1, 3)
    lp = lam_params.astype(jnp.float32)
    lam = jnp.exp(jnp.sum(lp[0] * lp[1])) - jnp.exp(jnp.sum(lp[2] * lp[3])) + lambda_init
    scale = d ** -0.5
    nb = S // Q_BLOCK
    qb = q.reshape(B_, H, 2, nb, Q_BLOCK, d).transpose(3, 0, 1, 2, 4, 5)

    def block(qblk):
        s = jnp.einsum('bhmqd,bhmkd->bhmqk', qblk, k).astype(jnp.float32) * scale
        p = jax.nn.softmax(s, axis=-1)
        w = p[:, :, 0] - lam * p[:, :, 1]
        return jnp.einsum('bhqk,bhkv->bhqv', w.astype(v.dtype), v)

    o = lax.map(block, qb)
    o = o.transpose(1, 0, 3, 2, 4).reshape(B_, S, H, 2 * d)
    o = rmsnorm(o, subln_g) * (1.0 - lambda_init)
    return o.reshape(B_, S, H * 2 * d)

def neighbourhood_attention(q, k, v, qk_norm, rpb):
    B_, S, H, d = q.shape
    rows = S // GRID_W
    kr = min(NA_ROWS, rows)
    q = rmsnorm(q, qk_norm[0])
    k = rmsnorm(k, qk_norm[1])

    def to_grid(t):
        return t.reshape(B_, rows, GRID_W, H, d).transpose(1, 0, 3, 2, 4)

    qg, kg, vg = to_grid(q), to_grid(k), to_grid(v)
    col = jnp.arange(GRID_W)
    col_start = jnp.clip(col - NA_COLS // 2, 0, GRID_W - NA_COLS)
    col_in = (col[None, :] >= col_start[:, None]) & (col[None, :] < col_start[:, None] + NA_COLS)
    dc_idx = jnp.clip(col[None, :] - col[:, None] + NA_COLS - 1, 0, 2 * NA_COLS - 2)
    scale = d ** -0.5

    def row_block(args):
        qr, r = args
        rs = jnp.clip(r - kr // 2, 0, rows - kr)
        kb = lax.dynamic_slice_in_dim(kg, rs, kr, axis=0)
        vb = lax.dynamic_slice_in_dim(vg, rs, kr, axis=0)
        s = jnp.einsum('bhqd,rbhkd->bhqrk', qr, kb).astype(jnp.float32) * scale
        dr_idx = rs + jnp.arange(kr) - r + NA_ROWS - 1
        bias = rpb[:, dr_idx][:, :, dc_idx].transpose(0, 2, 1, 3)
        s = s + bias[None].astype(jnp.float32)
        s = jnp.where(col_in[:, None, :], s, NEG_INF)
        p = jax.nn.softmax(s.reshape(B_, H, GRID_W, kr * GRID_W), axis=-1)
        p = p.reshape(B_, H, GRID_W, kr, GRID_W).astype(vb.dtype)
        return jnp.einsum('bhqrk,rbhkd->bhqd', p, vb)

    o = lax.map(row_block, (qg, jnp.arange(rows)))
    return o.transpose(1, 0, 3, 2, 4).reshape(B_, S, H * d)

def even_mixer(h, w_in, w_out, a_qk_norm, a_lambda, a_subln, b_qk_norm, b_rpb, lambda_init):
    B_, S, _ = h.shape
    u = h @ w_in
    qa, ka, va, qb, kb, vb = jnp.split(u, 6, axis=-1)
    oa = diff_attention(qa.reshape(B_, S, A_HEADS, 2, HEAD_DIM),
                        ka.reshape(B_, S, A_HEADS, 2, HEAD_DIM),
                        va.reshape(B_, S, A_HEADS, A_VDIM),
                        a_qk_norm, a_lambda, a_subln, lambda_init)
    ob = neighbourhood_attention(qb.reshape(B_, S, B_HEADS, HEAD_DIM),
                                 kb.reshape(B_, S, B_HEADS, HEAD_DIM),
                                 vb.reshape(B_, S, B_HEADS, HEAD_DIM),
                                 b_qk_norm, b_rpb)
    return jnp.concatenate([oa, ob], axis=-1) @ w_out

def multiscale_pool(h, w_grp, b_grp, scale):
    B_, S, D = h.shape
    hf = h.astype(jnp.float32)
    cs = jnp.concatenate([jnp.zeros((B_, 1, D), jnp.float32), jnp.cumsum(hf, axis=1)], axis=1)
    t = jnp.arange(S)
    outs = []
    for g, w in enumerate(POOL_WINDOWS):
        lo = jnp.clip(t - w // 2, 0, S)
        hi = jnp.clip(t - w // 2 + w, 0, S)
        csg = cs[:, :, g * POOL_GROUP_DIM:(g + 1) * POOL_GROUP_DIM]
        seg = jnp.take(csg, hi, axis=1) - jnp.take(csg, lo, axis=1)
        outs.append(seg / (hi - lo).astype(jnp.float32)[None, :, None])
    pooled = jnp.concatenate(outs, axis=-1)
    y = (pooled - hf).astype(h.dtype).reshape(B_, S, POOL_GROUPS, POOL_GROUP_DIM)
    y = jnp.einsum('bsgi,gio->bsgo', y, w_grp).reshape(B_, S, D) + b_grp
    return y * scale

def setup_inputs(seed: int = 0) -> dict:
    key = jax.random.key(seed)
    ks = jax.random.split(key, 17)

    def nrm(k, shape, s):
        return jax.random.normal(k, shape, jnp.float32) * s

    return {
        "x": nrm(ks[0], (BATCH, SEQ, D_MODEL), 1.0),
        "c": nrm(ks[1], (BATCH, D_MODEL), 1.0),
        "ada_w": nrm(ks[2], (DEPTH, D_MODEL, N_MOD * D_MODEL), 0.02),
        "ada_b": nrm(ks[3], (DEPTH, N_MOD * D_MODEL), 0.02),
        "norm_g": 1.0 + nrm(ks[4], (DEPTH, 3, D_MODEL), 0.02),
        "ff_w13": nrm(ks[5], (DEPTH, 2, D_MODEL, 2 * D_FF), D_MODEL ** -0.5),
        "ff_w2": nrm(ks[6], (DEPTH, 2, D_FF, D_MODEL), D_FF ** -0.5),
        "w_in": nrm(ks[7], (N_EVEN, D_MODEL, IN_WIDTH), D_MODEL ** -0.5),
        "w_out": nrm(ks[8], (N_EVEN, MIX_WIDTH, D_MODEL), MIX_WIDTH ** -0.5),
        "a_qk_norm": 1.0 + nrm(ks[9], (N_EVEN, 2, HEAD_DIM), 0.02),
        "a_lambda": nrm(ks[10], (N_EVEN, 4, HEAD_DIM), 0.1),
        "a_subln": 1.0 + nrm(ks[11], (N_EVEN, A_VDIM), 0.02),
        "b_qk_norm": 1.0 + nrm(ks[12], (N_EVEN, 2, HEAD_DIM), 0.02),
        "b_rpb": nrm(ks[13], (N_EVEN, B_HEADS, 2 * NA_ROWS - 1, 2 * NA_COLS - 1), 0.1),
        "pool_w": nrm(ks[14], (N_ODD, POOL_GROUPS, POOL_GROUP_DIM, POOL_GROUP_DIM), POOL_GROUP_DIM ** -0.5),
        "pool_b": nrm(ks[15], (N_ODD, D_MODEL), 0.02),
        "pool_scale": 1.0 + nrm(ks[16], (N_ODD, D_MODEL), 0.1),
    }

def reference(x, c, ada_w, ada_b, norm_g, ff_w13, ff_w2, w_in, w_out, a_qk_norm, a_lambda,
              a_subln, b_qk_norm, b_rpb, pool_w, pool_b, pool_scale):
    B_, S, D = x.shape
    cond = jax.nn.silu(c)
    for layer in range(DEPTH):
        mod = (cond @ ada_w[layer] + ada_b[layer]).reshape(B_, N_MOD, D)
        sh1, sc1, g1, sh2, sc2, g2, sh3, sc3, g3 = [mod[:, i] for i in range(N_MOD)]
        h = modulate(rmsnorm(x, norm_g[layer, 0]), sh1, sc1)
        x = x + 0.5 * g1[:, None, :] * swiglu(h, ff_w13[layer, 0], ff_w2[layer, 0])
        h = modulate(rmsnorm(x, norm_g[layer, 1]), sh2, sc2)
        if layer % 2 == 0:
            e = layer // 2
            lambda_init = 0.8 - 0.6 * math.exp(-0.3 * layer)
            mix = even_mixer(h, w_in[e], w_out[e], a_qk_norm[e], a_lambda[e], a_subln[e],
                             b_qk_norm[e], b_rpb[e], lambda_init)
        else:
            o = layer // 2
            mix = multiscale_pool(h, pool_w[o], pool_b[o], pool_scale[o])
        x = x + g2[:, None, :] * mix
        h = modulate(rmsnorm(x, norm_g[layer, 2]), sh3, sc3)
        x = x + 0.5 * g3[:, None, :] * swiglu(h, ff_w13[layer, 1], ff_w2[layer, 1])
    return x


_drawn_inputs = setup_inputs


def setup_inputs(seed=0):
    import zlib

    import numpy as np

    out = dict(_drawn_inputs(seed))
    spreads = {}
    factors = {'norm_g': 5.25,
     'a_qk_norm': 8.0,
     'a_lambda': 4.857,
     'a_subln': 35.273,
     'b_qk_norm': 8.0,
     'b_rpb': 25.105,
     'pool_b': 54.131,
     'pool_scale': 3.188}
    for name, (base, spread) in spreads.items():
        noise = np.random.default_rng([zlib.crc32(name.encode()), seed]).standard_normal(out[name].shape)
        drawn = base * np.exp(spread * noise) if base else spread * noise
        out[name] = __import__('jax').numpy.asarray(drawn.astype(out[name].dtype))
    for name, factor in factors.items():
        out[name] = (out[name] * factor).astype(out[name].dtype)
    return out
```

```python
import math
from contextlib import ExitStack

import numpy as np

import concourse.bass as bass
from concourse import mybir

P = 128
D = 1024
SEQ = 256
TT = SEQ // P
KT = D // P
DFF = 2816
NC = DFF // P
NMOD = 9
HD = 64
A_HEADS = 4
B_HEADS = 8
GRID_W = 64
ROWS = SEQ // GRID_W
NA_ROWS, NA_COLS = 8, 16
EPS = 1e-6
NEG = -1e30
LAM0 = 0.8 - 0.6 * math.exp(0.0)
SCALE = HD ** -0.5
WINDOWS = (2, 4, 8, 16)

F32 = mybir.dt.float32
F32R = mybir.dt.float32r
BF16 = mybir.dt.bfloat16
ACT = mybir.ActivationFunctionType
ALU = mybir.AluOpType
AX = mybir.AxisListType

FFN_PAIR = [0, 19, 30, 42]
WIN_PAIR, WOUT_PAIR, POOL_PAIR = 11, 17, 41
ADA_RING = 4
SUB_OF_FFN = [0, 2, 3, 5]
GATES = [NMOD * (s // 3) + 3 * (s % 3) + 2 for s in range(6)]
MOD_BANK = 6
H32 = [0, 8, 16, 24, None, 32]
HLO = [0, 8, 24, 32, 40, 48]
RS_AT = [0, 2, 10, 12, 14, 16]
POOL_STEPS = [13, 17, 22, 28]
WIN_SEGS = [(seg, half) for seg in ("qa", "ka", "va", "qb", "kb", "vb") for half in range(2)]
TP_MIX = 20


def norm_bank(s, j):
    return ([5, 0, 1, 2] if s == 0 else [5, 6, 0, 1])[j // 2]


def TP_HEAD(k):
    return 4 + k if k < A_HEADS else 8 + k


def slot_free(u):
    before = u - 4
    head = before // 2 if before < 2 * A_HEADS else before - 2 * A_HEADS + A_HEADS
    return TP_HEAD(head) + 1


def w2_count(Q):
    return Q + Q // NC + 2


def row_bcast(src, n):
    return bass.AP(tensor=src.tensor, offset=src.offset, ap=[[0, P], [1, n]])


def hpad(arena):
    return arena[:, 0:KT * (SEQ + 16)].rearrange("p (j n) -> p j n", j=KT)


def pool_tmp(arena):
    base, w = KT * (SEQ + 16), 2 * (SEQ + 16)
    return [arena[:, base + i * w:base + (i + 1) * w].rearrange("p (j n) -> p j n", j=2) for i in range(2)]


def pool_y(arena, g):
    base = (KT + 4) * (SEQ + 16) + g * 2 * SEQ
    return arena[:, base:base + 2 * SEQ].rearrange("p (j n) -> p j n", j=2)


def build_program(nc, x_in, c_col, ada_w, ada_bT, norm_gT, ff_w13, ff_w2, w_in, w_out, a_qk_norm,
                  a_lambda, a_subln, b_qk_norm, b_rpb, pool_w, pool_b, pool_scale,
                  rope_cs, inv_count, identity, exchange, out):
    ctx = ExitStack()
    with ctx:
        def sb(name, shape, dt=F32):
            return ctx.enter_context(nc.sbuf_tensor(name, shape, dt))

        def sem(name):
            return ctx.enter_context(nc.semaphore(name))

        raw13 = sb("raw13", [P, 2, 2, KT, 256])
        raw2 = sb("raw2", [P, 2, D])
        hi13 = sb("hi13", [P, 2, 2048], F32R)
        lo13 = sb("lo13", [P, 2, 2048], F32R)
        hi2 = sb("hi2", [P, 2, D], F32R)
        lo2 = sb("lo2", [P, 2, D], F32R)
        ada = sb("ada", [P, ADA_RING, D])
        acc = sb("acc", [P, D])
        x = sb("x", [P, TT, D])
        xn = sb("xn", [P, TT, D])
        hT_hi = sb("hT_hi", [P, KT, SEQ], F32R)
        hT_lo = sb("hT_lo", [P, KT, SEQ], F32R)
        gate = sb("gate", [P, D])
        s_buf = sb("s_buf", [P, 2, SEQ])
        u_buf = sb("u_buf", [P, 2, SEQ])
        u_hi = sb("u_hi", [P, 2, SEQ], F32R)
        u_lo = sb("u_lo", [P, 2, SEQ], F32R)
        arena = sb("arena", [P, 12288])
        bias = arena[:, 0:4096].rearrange("p (t h r c) -> p t h r c", t=TT, h=B_HEADS, r=ROWS)
        qkT = arena[:, 4096:6144].rearrange("p (b n) -> p b n", b=8)
        h32 = qkT
        v_sb = arena[:, 6144:8192].rearrange("p (t n) -> p t n", t=TT)
        mix = arena[:, 8192:10240].rearrange("p (t n) -> p t n", t=TT)
        e_buf = arena[:, 10240:12288].rearrange("p (s t n) -> p s t n", s=4, t=TT)
        modc = sb("modc", [P, 2 * NMOD, KT])
        mraw = sb("mraw", [P, 1, KT])
        adab = sb("adab", [P, 2 * NMOD, KT])
        ngT = sb("ngT", [P, 6, KT])
        acol = sb("acol", [P, 6, KT])
        cond = sb("cond", [P, KT])
        ident = sb("ident", [P, P])
        ones = sb("ones", [P, P])
        zeros = sb("zeros", [P, P], BF16)
        exch = sb("exch", [P, P])
        neg_half = sb("neg_half", [P, 16])
        ss = sb("ss", [P, 16])
        rstd = sb("rstd", [P, 16])
        gnorm = sb("gnorm", [P, 2, 2, HD])
        rope = arena[:, 10240:10368].rearrange("p (c t d) -> p c t d", c=2, t=TT)
        lamb = arena[:, 10368:10624].rearrange("p (a d) -> p a d", a=4)
        subln = sb("subln", [P, P])
        lam = sb("lam", [P, 4])
        nmx = sb("nmx", [P, 16, TT])
        esum = sb("esum", [P, 16, TT])
        erec = sb("erec", [P, 16, TT])
        rope_g = sb("rope_g", [P, 2, TT, 2, HD])
        ps = ctx.enter_context(nc.psum_tensor("ps", [P, 8, 512], F32))

        ptT = [s_buf, u_buf]

        raw13_in = [sem(f"raw13_in{i}") for i in range(2)]
        raw2_in = [sem(f"raw2_in{i}") for i in range(2)]
        ada_in = [sem(f"ada_in{i}") for i in range(ADA_RING)]
        hi13_done, lo13_done, unit_used = sem("hi13_done"), sem("lo13_done"), sem("unit_used")
        hi2_done, lo2_done, w2_used = sem("hi2_done"), sem("lo2_done"), sem("w2_used")
        y0_done = sem("y0_done")
        silu_done, u_done = sem("silu_done"), sem("u_done")
        uhi_done, ulo_done = sem("uhi_done"), sem("ulo_done")
        ada_used, mod_ps, mod_red, mod_done = sem("ada_used"), sem("mod_ps"), sem("mod_red"), sem("mod_done")
        diag_done, gate_ps, gate_ready = sem("diag_done"), sem("gate_ps"), sem("gate_ready")
        x_tmp, x_done = sem("x_tmp"), sem("x_done")
        ss_done, rstd_tmp, rstd_done, xn_done = sem("ss_done"), sem("rstd_tmp"), sem("rstd_done"), sem("xn_done")
        xT_done, acol_done = sem("xT_done"), sem("acol_done")
        h32_done, hhi_done, hlo_done = sem("h32_done"), sem("hhi_done"), sem("hlo_done")
        ident_in = sem("ident_in")
        small_in, x_in_sem, cond_done = sem("small_in"), sem("x_in_sem"), sem("cond_done")
        setup_done, half_set, bias_in, bias_done = sem("setup_done"), sem("half_set"), sem("bias_in"), sem("bias_done")
        lam_done, setup_step = sem("lam_done"), sem("setup_step")
        win_out = sem("win_out")
        sq_done, qred_done, qk_step, qk_done = sem("sq_done"), sem("qred_done"), sem("qk_step"), sem("qk_done")
        tp_fill, tp_out = sem("tp_fill"), sem("tp_out")
        score_done, nmx_tmp, nmx_done, exp_done = sem("score_done"), sem("nmx_tmp"), sem("nmx_done"), sem("exp_done")
        erec_done, comb_tmp, comb_done, pv_done = sem("erec_done"), sem("comb_tmp"), sem("comb_done"), sem("pv_done")
        osq_done, ored_done, omul_done, mix_done = sem("osq_done"), sem("ored_done"), sem("omul_done"), sem("mix_done")
        pool_in, pool_step, pooled_hi = sem("pool_in"), sem("pool_step"), sem("pooled_hi")
        out_sem = sem("out_sem")

        def raw13_count(pair):
            return 32 * (pair // 2 + 1)

        w13_v = [ff_w13[f // 2, f % 2].rearrange("(k p) n -> p k n", p=P) for f in range(4)]
        w2_v = [ff_w2[f // 2, f % 2].rearrange("(c p) n -> p c n", p=P) for f in range(4)]
        win_v = w_in[0].rearrange("(k p) n -> p k n", p=P)
        wout_v = w_out[0].rearrange("(k p) n -> p k n", p=P)
        pw_v = pool_w[0].rearrange("g (k p) n -> p (g k) n", p=P)
        ada_v = [ada_w[l].rearrange("(j p) n -> p j n", p=P) for l in range(2)]
        out_v = out[0].rearrange("(t p) n -> p t n", p=P)
        x_v = x_in[0].rearrange("(t p) n -> p t n", p=P)

        def unit_src(n):
            pair, half = n // 2, n % 2
            slot = pair % 2
            for f in range(4):
                if FFN_PAIR[f] <= pair < FFN_PAIR[f] + 11:
                    src = raw13[:, slot, :, :, half * P:half * P + P].rearrange("p h k n -> p (h k) n")
                    return src, [t[:, half, :].rearrange("p (a n) -> p a n", n=P) for t in (hi13, lo13)]
            if pair == POOL_PAIR:
                return (raw13[:, slot, half, 0:4, :].rearrange("p k n -> p (k n)"),
                        [t[:, half, 0:1024] for t in (hi13, lo13)])
            return (raw13[:, slot, half, :, :].rearrange("p k n -> p (k n)"),
                    [t[:, half, :] for t in (hi13, lo13)])

        block = ctx.enter_context(nc.Block())

        @block.sync
        def _(sp):
            def free13(pair):
                if pair >= 2:
                    sp.wait_ge(lo13_done, 2 * (pair - 2) + 2)

            def load_pair(pair, srcs):
                free13(pair)
                for h in range(2):
                    dst = raw13[:, pair % 2, h, 0:srcs[h].shape[1], :]
                    sp.dma_start(dst, srcs[h]).then_inc(raw13_in[pair % 2], 16)

            def load_w2(f, q):
                n = NC * f + q
                if n >= 2:
                    sp.wait_ge(lo2_done, n - 1)
                sp.dma_start(raw2[:, n % 2, :], w2_v[f][:, q, :]).then_inc(raw2_in[n % 2], 16)

            sp.dma_start(x[:, 0, :], x_v[:, 0, :]).then_inc(x_in_sem, 16)
            sp.dma_start(x[:, 1, :], x_v[:, 1, :]).then_inc(x_in_sem, 16)
            for f in range(4):
                base = FFN_PAIR[f]
                for e in range(2):
                    if f == 0 and e == 1:
                        sp.wait_ge(ada_used, 2 * KT - 4)
                        load_w2(0, 0)
                    load_pair(base + e, [w13_v[f][:, :, h * DFF + e * 256:h * DFF + e * 256 + 256]
                                         for h in range(2)])
                    if f > 0 or e == 1:
                        load_w2(f, e)

                def turn(i):
                    for e in range(2):
                        pair = base + 2 + e
                        sp.wait_ge(lo13_done, 4 * i + (2 * pair - 2))
                        for h in range(2):
                            sp.dma_start(raw13[:, pair % 2, h, :, :],
                                         w13_v[f][:, :, bass.ds(i * 512 + (h * DFF + (2 + e) * 256), 256)]
                                         ).then_inc(raw13_in[pair % 2], 16)
                        for g in range(2):
                            load_w2_turn(i, 2 + 2 * e + g)

                def load_w2_turn(i, q):
                    n = NC * f + q
                    sp.wait_ge(lo2_done, 4 * i + (n - 1))
                    sp.dma_start(raw2[:, n % 2, :],
                                 w2_v[f][:, bass.ds(4 * i + q, 1), :].rearrange("p a n -> p (a n)")
                                 ).then_inc(raw2_in[n % 2], 16)

                with sp.Fori(0, 4) as i:
                    turn(i)
                load_pair(base + 10, [w13_v[f][:, :, h * DFF + 2560:h * DFF + 2816] for h in range(2)])
                for q in range(18, NC):
                    load_w2(f, q)
                if f == 0:
                    for t in range(TT):
                        for half in range(2):
                            rq = 2 * t + half
                            for rk in range(ROWS):
                                off = (rk - rq + NA_ROWS - 1) * (2 * NA_COLS - 1) + NA_COLS - GRID_W
                                src = bass.AP(tensor=b_rpb.tensor, offset=off,
                                              ap=[[1, 64], [(2 * NA_ROWS - 1) * (2 * NA_COLS - 1), B_HEADS], [1, GRID_W]])
                                sp.dma_start(bias[half * 64:half * 64 + 64, t, :, rk, :], src).then_inc(bias_in, 16)
                    for w in range(6):
                        load_pair(WIN_PAIR + w, [win_v[:, :, c:c + 256] for c in (512 * w, 512 * w + 256)])
                    for w in range(2):
                        load_pair(WOUT_PAIR + w, [wout_v[:, :, w * 512 + h * 256:w * 512 + h * 256 + 256]
                                                  for h in range(2)])
                if f == 2:
                    load_pair(POOL_PAIR, [pw_v[:, 4 * h:4 * h + 4, :] for h in range(2)])
            for t in range(TT):
                sp.wait_ge(x_done, 2 * 5 + t + 1)
                sp.dma_start(out_v[:, t, :], x[:, t, :]).then_inc(out_sem, 16)
            sp.wait_ge(out_sem, 32)

        @block.gpsimd
        def _(pool):
            def ada_vector(g, first=0, last=KT):
                for j in range(first, last):
                    n = KT * g + j
                    if n >= ADA_RING:
                        pool.wait_ge(ada_used, n - ADA_RING + 1)
                    pool.dma_start(ada[:, j % ADA_RING, :], ada_v[0][:, j, g * D:(g + 1) * D]
                                   ).then_inc(ada_in[j % ADA_RING], 16)

            ada_vector(0, 0, ADA_RING)
            nc.gpsimd.memset(neg_half[:, :], -0.5).then_inc(half_set, 1)
            def rms(width, wait_sem, wait_at, cols, tmp_at):
                pool.wait_ge(wait_sem, wait_at)
                nc.gpsimd.tensor_scalar(rstd[:, cols], ss[:, cols], 1.0 / width, EPS, ALU.mult, ALU.add
                                        ).then_inc(rstd_tmp, 1)
                pool.wait_ge(rstd_tmp, tmp_at)
                nc.gpsimd.tensor_tensor(rstd[:, cols], rstd[:, cols], neg_half[:, cols], ALU.pow
                                        ).then_inc(rstd_done, 1)

            rms_n = [0]

            def next_rms(width, wait_sem, wait_at, cols):
                rms_n[0] += 1
                rms(width, wait_sem, wait_at, cols, rms_n[0])

            pool.wait_ge(half_set, 1)
            for t in range(TT):
                next_rms(D, ss_done, t + 1, slice(t, t + 1))
            ada_vector(0, ADA_RING, KT)
            ada_vector(1)
            def ada_loop(layer, m0, done, turns):
                with pool.Fori(0, turns) as i:
                    for j in range(KT):
                        pool.wait_ge(ada_used, KT * i + (KT * done + j - ADA_RING + 1))
                        pool.dma_start(ada[:, j % ADA_RING, :],
                                       ada_v[layer][:, j, bass.ds(i * D + m0 * D, D)]
                                       ).then_inc(ada_in[j % ADA_RING], 16)

            def norm_rms(s):
                for t in range(TT):
                    next_rms(D, ss_done, 2 * s + t + 1, slice(t, t + 1))

            ada_loop(0, 2, 2, 5)
            norm_rms(1)
            ada_vector(7)
            pool.wait_ge(bias_in, 16 * TT * 2 * ROWS)
            step = [0]
            for t in range(TT):
                for half in range(2):
                    rows = slice(half * 64, half * 64 + 64)
                    low = bias[rows, t, :, :, 0:48].rearrange("p h r c -> p (h r) c")
                    high = bias[rows, t, :, :, 16:64].rearrange("p h r c -> p (h r) c")
                    nc.gpsimd.affine_select(out=low, in_=low, compare_op=ALU.is_ge, fill=NEG,
                                            base=NA_COLS // 2 - (GRID_W - 1),
                                            pattern=[[0, 32], [1, 48]], channel_multiplier=1).then_inc(bias_done, 1)
                    step[0] += 1
                    pool.wait_ge(bias_done, step[0])
                    nc.gpsimd.affine_select(out=high, in_=high, compare_op=ALU.is_ge, fill=NEG,
                                            base=NA_COLS // 2 - 1 - NA_COLS + (GRID_W - 1),
                                            pattern=[[0, 32], [-1, 48]], channel_multiplier=-1).then_inc(bias_done, 1)
                    step[0] += 1
                    pool.wait_ge(bias_done, step[0])
            ada_vector(8)
            for n in range(2 * TT):
                next_rms(HD, qred_done, n + 1, slice(0, 16))
            for t in range(TT):
                next_rms(P, ored_done, t + 1, slice(4 * t, 4 * t + 4))
            norm_rms(2)
            ada_loop(1, 0, 9, 5)
            norm_rms(3)
            ada_loop(1, 5, 14, 4)
            for n, src in enumerate((pool_b, pool_scale)):
                if n == 0:
                    pool.wait_ge(x_done, 2 * TT)
                pool.dma_start(v_sb[:, n, :], row_bcast(src, D)).then_inc(pool_in, 16)
            pool.dma_start(mix[:, 0, 0:SEQ * 4].rearrange("p (w t) -> p w t", w=4),
                           bass.AP(tensor=inv_count.tensor, offset=inv_count.offset,
                                   ap=[[0, P], [SEQ, 4], [1, SEQ]])).then_inc(pool_in, 16)
            norm_rms(4)
            norm_rms(5)

        @block.scalar
        def _(act):
            def split_hi(n, i=0):
                act.wait_ge(raw13_in[(n // 2) % 2], 32 * i + raw13_count(n // 2))
                if n >= 2:
                    act.wait_ge(unit_used, 4 * i + (n - 1))
                src, (hi, _) = unit_src(n)
                nc.scalar.activation(hi, src, ACT.Copy).then_inc(hi13_done, 1)

            def norm_squares(s):
                for t in range(TT):
                    if s == 0:
                        act.wait_ge(x_in_sem, 32)
                    else:
                        act.wait_ge(x_done, 2 * (s - 1) + t + 1)
                    nc.scalar.activation(xn[:, t, :], x[:, t, :], ACT.Square, accum_out=ss[:, t:t + 1]
                                         ).then_inc(ss_done, 1)

            def norm_out(s):
                g = NMOD * (s // 3) + 3 * (s % 3)
                act.wait_ge(acol_done, s + 1)
                for j in range(KT):
                    if j % 2 == 0:
                        act.wait_ge(xT_done, 4 * s + j // 2 + 1)
                    nc.scalar.activation(h32[:, j, :], ps[:, norm_bank(s, j), (j % 2) * 256:(j % 2) * 256 + 256],
                                         ACT.Identity, bias=modc[:, g, j:j + 1], scale=acol[:, s, j:j + 1]
                                         ).then_inc(h32_done, 1)

            def gate_copy(k):
                act.wait_ge(gate_ps, k + 1)
                nc.scalar.activation(gate[:, :], ps[:, 6:8, :].rearrange("p b n -> p (b n)"), ACT.Copy
                                     ).then_inc(gate_ready, 1)

            def silu(Q, n, i4=0):
                act.wait_ge(unit_used, i4 + (n + 1))
                nc.scalar.activation(s_buf[:, Q % 2, :], ps[:, 4 + Q % 2, 0:256], ACT.Silu).then_inc(silu_done, 1)

            def u_high(Q, i4=0):
                act.wait_ge(u_done, i4 + (Q + 1))
                nc.scalar.activation(u_hi[:, Q % 2, :], u_buf[:, Q % 2, :], ACT.Copy).then_inc(uhi_done, 1)

            def w2_high(Q, i=0):
                act.wait_ge(raw2_in[Q % 2], 32 * i + 16 * (Q // 2 + 1))
                if Q >= 1:
                    act.wait_ge(w2_used, 4 * i + (Q + Q // NC))
                nc.scalar.activation(hi2[:, Q % 2, :], raw2[:, Q % 2, :], ACT.Copy).then_inc(hi2_done, 1)

            def ffn(f):
                Q0, n0 = NC * f, 2 * FFN_PAIR[f]
                w2_high(Q0)
                split_hi(n0 + 1)
                with act.Fori(0, 5) as i:
                    for q in range(1, 5):
                        silu(Q0 + q - 1, n0 + q - 1, 4 * i)
                        w2_high(Q0 + q, i)
                        u_high(Q0 + q - 1, 4 * i)
                        split_hi(n0 + q + 1, i)
                silu(Q0 + 20, n0 + 20)
                w2_high(Q0 + 21)
                u_high(Q0 + 20)
                silu(Q0 + 21, n0 + 21)
                u_high(Q0 + 21)
                gate_copy(SUB_OF_FFN[f])
                if f < 3:
                    split_hi(n0 + 22)

            act.dma_start(cond[:, :], c_col).then_inc(cond_done, 16)
            act.dma_start(ident[:, :], identity).then_inc(ident_in, 16)
            act.dma_start(exch[:, :], exchange).then_inc(small_in, 16)
            act.dma_start(adab[:, :, :], ada_bT).then_inc(small_in, 16)
            act.dma_start(ngT[:, :, :], norm_gT).then_inc(small_in, 16)
            for n, src in enumerate((a_qk_norm, b_qk_norm)):
                act.dma_start(gnorm[:, n, :, :].rearrange("p a b -> p (a b)"), row_bcast(src, 2 * HD)
                              ).then_inc(small_in, 16)
            act.dma_start(rope[:, :, :, :], rope_cs).then_inc(small_in, 16)
            act.dma_start(subln[:, :], row_bcast(a_subln, P)).then_inc(small_in, 16)
            act.dma_start(lamb[:, :, :].rearrange("p a b -> p (a b)"), row_bcast(a_lambda, 4 * HD)
                          ).then_inc(small_in, 16)
            act.wait_ge(cond_done, 16)
            nc.scalar.activation(cond[:, :], cond[:, :], ACT.Silu).then_inc(cond_done, 1)
            norm_squares(0)
            split_hi(0)
            norm_out(0)
            ffn(0)
            norm_squares(1)
            norm_out(1)
            act.wait_ge(lam_done, 1)
            nc.scalar.activation(lam[:, 2:4], lam[:, 0:2], ACT.Exp).then_inc(lam_done, 1)

            def win_evac(w):
                n = 2 * WIN_PAIR + w
                act.wait_ge(unit_used, n + 1)
                seg, half = WIN_SEGS[w]
                if seg in ("va", "vb"):
                    c0 = (512 if seg == "vb" else 0) + half * 256
                    dst = v_sb[:, :, c0:c0 + 256]
                else:
                    c0 = (512 if seg[0] == "k" else 0) + half * 256
                    dst = xn[:, :, c0:c0 + 256]
                    if seg == "qb" and half == 0:
                        act.wait_ge(tp_fill, 4)
                nc.scalar.activation(dst, ps[:, 4 + w % 2, :].rearrange("p (t n) -> p t n", t=TT), ACT.Copy
                                     ).then_inc(win_out, 1)

            tp = [0]

            def tp_evac(dst):
                tp[0] += 1
                act.wait_ge(tp_fill, tp[0])
                nc.scalar.activation(dst, ps[:, (tp[0] - 1) % 2, :], ACT.Copy).then_inc(tp_out, 1)

            def qk_evac():
                for b in range(4):
                    tp_evac(qkT[:, 2 * b:2 * b + 2, :].rearrange("p b n -> p (b n)"))

            def squares(n):
                if n >= 1:
                    act.wait_ge(qred_done, n)
                act.wait_ge(win_out, 4 if n < 2 else 10)
                nc.scalar.activation(gate[:, :], xn[:, n % 2, :], ACT.Square).then_inc(sq_done, 1)

            def exps(u):
                act.wait_ge(nmx_done, u + 1)
                if u >= 4:
                    act.wait_ge(tp_fill, slot_free(u))
                for t in range(TT):
                    nc.scalar.activation(e_buf[:, u % 4, t, :], ps[:, 6 + u % 2, t * 256:t * 256 + 256], ACT.Exp,
                                         bias=nmx[:, u, t:t + 1], accum_out=esum[:, u, t:t + 1]).then_inc(exp_done, 1)

            def weights_evac(k):
                if k >= 2:
                    act.wait_ge(pv_done, k - 1)
                tp_evac(ptT[k % 2][:, :, :].rearrange("p a n -> p (a n)"))

            n0 = 2 * WIN_PAIR
            for w in range(12):
                split_hi(n0 + w + 1)
                win_evac(w)
                if w == 3:
                    squares(0)
                if w == 4:
                    squares(1)
                if w == 5:
                    qk_evac()
                if 6 <= w < 10:
                    h = w - 6
                    if h >= 1:
                        weights_evac(h - 1)
                    exps(2 * h)
                    exps(2 * h + 1)
                if w == 10:
                    weights_evac(3)
                    squares(2)
                if w == 11:
                    squares(3)
            split_hi(n0 + 13)
            for t in range(TT):
                act.wait_ge(pv_done, A_HEADS)
                nc.scalar.activation(mix[:, t, 0:512], ps[:, 2 + t, :], ACT.Square).then_inc(osq_done, 1)
            qk_evac()
            for b in range(B_HEADS + 1):
                if b < B_HEADS:
                    exps(8 + b)
                if b >= 1:
                    weights_evac(3 + b)
            for j2 in range(4):
                tp_evac(h32[:, 2 * j2:2 * j2 + 2, :].rearrange("p j n -> p (j n)"))
            gate_copy(1)
            for n in (36, 37, 38):
                split_hi(n)
            norm_squares(2)
            norm_out(2)
            ffn(1)
            norm_squares(3)
            norm_out(3)
            ffn(2)
            norm_squares(4)
            split_hi(83)
            for g in range(4):
                act.wait_ge(pool_step, POOL_STEPS[g])
                nc.scalar.activation(hT_hi[:, 2 * g:2 * g + 2, :], pool_y(arena, g), ACT.Copy).then_inc(pooled_hi, 1)
            split_hi(84)
            gate_copy(4)
            norm_squares(5)
            norm_out(5)
            ffn(3)

        @block.vector
        def _(dve):
            V = nc.vector

            def split_lo(n, i4=0, part=None):
                dve.wait_ge(hi13_done, i4 + (n + 1))
                src, (hi, lo) = unit_src(n)
                if part is not None:
                    half = src.shape[1] // 2
                    src, hi, lo = (v[:, part * half:(part + 1) * half] for v in (src, hi, lo))
                ins = V.tensor_tensor(lo, src, hi.bitcast(F32), ALU.subtract)
                if part != 0:
                    ins.then_inc(lo13_done, 1)

            def w2_low(Q, i4=0):
                dve.wait_ge(hi2_done, i4 + (Q + 1))
                V.tensor_tensor(lo2[:, Q % 2, :], raw2[:, Q % 2, :], hi2[:, Q % 2, :].bitcast(F32), ALU.subtract
                                ).then_inc(lo2_done, 1)

            def u_mul(Q, i4=0):
                dve.wait_ge(silu_done, i4 + (Q + 1))
                V.tensor_tensor(u_buf[:, Q % 2, :], s_buf[:, Q % 2, :], ps[:, 4 + Q % 2, 256:512], ALU.mult
                                ).then_inc(u_done, 1)

            def u_low(Q, i4=0):
                dve.wait_ge(uhi_done, i4 + (Q + 1))
                V.tensor_tensor(u_lo[:, Q % 2, :], u_buf[:, Q % 2, :], u_hi[:, Q % 2, :].bitcast(F32), ALU.subtract
                                ).then_inc(ulo_done, 1)

            def ada_tile(g, j, i=0, gates=0):
                dve.wait_ge(ada_in[j % ADA_RING], 32 * i + 16 * ((KT * g + j) // ADA_RING + 1))
                w = ada[:, j % ADA_RING, :]
                if j == 0:
                    if gates:
                        dve.wait_ge(gate_ps, gates)
                    V.tensor_scalar(acc[:, :], w, cond[:, 0:1], None, ALU.mult).then_inc(ada_used, 1)
                else:
                    dve.wait_ge(ada_used, KT * i + (KT * g + j))
                    V.scalar_tensor_tensor(acc[:, :], w, cond[:, j:j + 1], acc[:, :], ALU.mult, ALU.add
                                           ).then_inc(ada_used, 1)

            def mod_out(g, i=0):
                dve.wait_ge(mod_ps, i + (g + 1))
                if isinstance(i, int):
                    dst, b = modc[:, g:g + 1, :], adab[:, g:g + 1, :]
                else:
                    dst, b = modc[:, bass.ds(i + g, 1), :], adab[:, bass.ds(i + g, 1), :]
                V.tensor_reduce(mraw[:, 0, :], ps[:, MOD_BANK:MOD_BANK + 2, :].rearrange("p b (k n) -> p (b k) n", n=P),
                                AX.X, ALU.add).then_inc(mod_red, 1)
                dve.wait_ge(mod_red, i + (g + 1))
                V.tensor_tensor(dst, mraw[:, :, :], b, ALU.add).then_inc(mod_done, 1)

            def diag(g, k, scale):
                dve.wait_ge(mod_done, g + 1)
                if k >= 1:
                    dve.wait_ge(gate_ps, k)
                for j in range(KT):
                    V.tensor_scalar(acc[:, j * P:(j + 1) * P], ident[:, :], modc[:, g, j:j + 1], scale,
                                    ALU.mult, ALU.mult).then_inc(diag_done, 1)

            def make_acol(s):
                g = NMOD * (s // 3) + 3 * (s % 3)
                dve.wait_ge(mod_done, g + 2)
                V.scalar_tensor_tensor(acol[:, s, :], modc[:, g + 1, :], 1.0, ngT[:, s, :], ALU.add, ALU.mult
                                       ).then_inc(acol_done, 1)

            def residual(s, k, sem_, at, y0=0):
                dve.wait_ge(gate_ready, k + 1)
                if y0:
                    dve.wait_ge(y0_done, y0)
                for t in range(TT):
                    if t == (1 if y0 else 0):
                        dve.wait_ge(sem_, at)
                    V.tensor_tensor(xn[:, t, :], ps[:, 2 * t:2 * t + 2, :].rearrange("p b n -> p (b n)"),
                                    gate[:, :], ALU.mult).then_inc(x_tmp, 1)
                    dve.wait_ge(x_tmp, 2 * (s - 1) + t + 1)
                    V.tensor_tensor(x[:, t, :], x[:, t, :], xn[:, t, :], ALU.add).then_inc(x_done, 1)

            def norm_scale(s):
                for t in range(TT):
                    dve.wait_ge(rstd_done, RS_AT[s] + t + 1)
                    V.tensor_scalar(xn[:, t, :], x[:, t, :], rstd[:, t:t + 1], None, ALU.mult).then_inc(xn_done, 1)

            def split_h(j2):
                h, hi, lo = (v[:, 2 * j2:2 * j2 + 2, :].rearrange("p j n -> p (j n)") for v in (h32, hT_hi, hT_lo))
                V.tensor_copy(hi, h).then_inc(hhi_done, 1)
                hhi_n[0] += 1
                dve.wait_ge(hhi_done, hhi_n[0])
                V.tensor_tensor(lo, h, hi.bitcast(F32), ALU.subtract).then_inc(hlo_done, 2)

            hhi_n = [0]

            def norm_split(s):
                for j2 in range(KT // 2):
                    dve.wait_ge(h32_done, H32[s] + 2 * j2 + 2)
                    split_h(j2)

            def norm(s, n=None):
                if n is not None:
                    split_lo(n, part=0)
                norm_scale(s)
                if n is not None:
                    split_lo(n, part=1)
                norm_split(s)

            def ffn(f, m0=None, turns=0, gates=0):
                Q0, n0 = NC * f, 2 * FFN_PAIR[f]
                w2_low(Q0)
                split_lo(n0 + 1)

                def body(i, with_ada):
                    for d in range(4):
                        Q = Q0 + 1 + d
                        u_mul(Q - 1, 4 * i)
                        if with_ada:
                            ada_tile(m0, 2 * d, i, gates)
                        u_low(Q - 1, 4 * i)
                        if with_ada:
                            ada_tile(m0, 2 * d + 1, i, gates)
                        w2_low(Q, 4 * i)
                        split_lo(n0 + d + 2, 4 * i)
                    if with_ada:
                        mod_out(m0, i)

                if turns:
                    with dve.Fori(0, turns) as i:
                        body(i, True)
                if turns == 0:
                    with dve.Fori(0, 5) as i:
                        body(i, False)
                elif turns < 5:
                    body(turns, False)
                u_mul(Q0 + 20)
                u_low(Q0 + 20)
                w2_low(Q0 + 21)
                diag(GATES[SUB_OF_FFN[f]], SUB_OF_FFN[f], 0.5)
                u_mul(Q0 + 21)
                u_low(Q0 + 21)

            V.memset(ones[:, :], 1.0).then_inc(setup_done, 1)
            V.memset(zeros[:, :], 0.0).then_inc(setup_done, 1)
            norm_scale(0)
            dve.wait_ge(cond_done, 17)
            for g in range(2):
                for j in range(KT):
                    ada_tile(g, j)
                if g == 0:
                    split_lo(0)
                    dve.wait_ge(small_in, 16 * 8)
                mod_out(g)
            make_acol(0)
            norm_split(0)
            ffn(0, m0=2, turns=5)
            V.tensor_scalar(gnorm[:, :, 0, :], gnorm[:, :, 0, :], SCALE, None, ALU.mult).then_inc(setup_step, 1)
            dve.wait_ge(setup_step, 1)
            for cs in range(2):
                for t in range(TT):
                    V.tensor_tensor(rope_g[:, cs, t, :, :].rearrange("p q (h d) -> p (q h) d", d=32),
                                    gnorm[:, 0, :, :].rearrange("p q (h d) -> p (q h) d", d=32),
                                    rope[:, cs, t, :].unsqueeze(1).to_broadcast([P, 4, 32]), ALU.mult
                                    ).then_inc(setup_step, 1)
            V.tensor_scalar(subln[:, :], subln[:, :], 1.0 - LAM0, None, ALU.mult).then_inc(setup_step, 1)
            V.tensor_tensor(lamb[:, 0:4:2, :], lamb[:, 0:4:2, :], lamb[:, 1:4:2, :], ALU.mult).then_inc(setup_step, 1)
            dve.wait_ge(setup_step, 7)
            V.tensor_reduce(lam[:, 0:2], lamb[:, 0:4:2, :], AX.X, ALU.add).then_inc(lam_done, 1)
            make_acol(1)
            residual(1, 0, w2_used, w2_count(NC - 1), y0=1)
            norm(1, 22)

            def qk_norm(t, ab, at):
                dve.wait_ge(sq_done, 2 * ab + t + 1)
                V.tensor_reduce(ss[:, 0:16], gate[:, :].rearrange("p (g d) -> p g d", d=HD), AX.X, ALU.add
                                ).then_inc(qred_done, 1)
                dve.wait_ge(rstd_done, at)
                qk = xn[:, t, :].rearrange("p (g d) -> p g d", d=HD)
                V.tensor_tensor(qk, qk, rstd[:, 0:16].unsqueeze(2).to_broadcast([P, 16, HD]), ALU.mult
                                ).then_inc(qk_step, 1)
                qk_n[0] += 1
                dve.wait_ge(qk_step, qk_n[0])
                qk4 = xn[:, t, :].rearrange("p (s h d) -> p s h d", s=2, h=8)
                if ab == 0:
                    for cs in range(2):
                        V.tensor_tensor(mix[:, cs, :].rearrange("p (s h d) -> p s h d", s=2, h=8), qk4,
                                        rope_g[:, cs, t, :, :].unsqueeze(2).to_broadcast([P, 2, 8, HD]), ALU.mult
                                        ).then_inc(qk_step, 1)
                    qk_n[0] += 2
                    dve.wait_ge(qk_step, qk_n[0])
                    xc = mix[:, 0, :].rearrange("p (g d) -> p g d", d=HD)
                    xs = mix[:, 1, :].rearrange("p (g d) -> p g d", d=HD)
                    V.tensor_tensor(qk[:, :, 0:32], xc[:, :, 0:32], xs[:, :, 32:64], ALU.subtract).then_inc(qk_done, 1)
                    V.tensor_tensor(qk[:, :, 32:64], xs[:, :, 0:32], xc[:, :, 32:64], ALU.add).then_inc(qk_done, 1)
                else:
                    V.tensor_tensor(qk4, qk4, gnorm[:, 1, :, :].unsqueeze(2).to_broadcast([P, 2, 8, HD]), ALU.mult
                                    ).then_inc(qk_done, 2)

            qk_n = [0]

            def row_max(u):
                dve.wait_ge(score_done, u + 1)
                V.tensor_reduce(nmx[:, u, :], ps[:, 6 + u % 2, :].rearrange("p (t n) -> p t n", t=TT), AX.X, ALU.max
                                ).then_inc(nmx_tmp, 1)
                dve.wait_ge(nmx_tmp, u + 1)
                V.tensor_scalar(nmx[:, u, :], nmx[:, u, :], -1.0, None, ALU.mult).then_inc(nmx_done, 1)

            def combine(h):
                dve.wait_ge(exp_done, 2 * (2 * h + 2))
                V.reciprocal(erec[:, 2 * h:2 * h + 2, :], esum[:, 2 * h:2 * h + 2, :]).then_inc(erec_done, 1)
                dve.wait_ge(erec_done, 2 * h + 1)
                V.tensor_scalar(erec[:, 2 * h + 1, :], erec[:, 2 * h + 1, :], lam[:, 0:1], None, ALU.mult
                                ).then_inc(erec_done, 1)
                dve.wait_ge(erec_done, 2 * h + 2)
                a, b = (2 * h) % 4, (2 * h + 1) % 4
                for t in range(TT):
                    V.tensor_scalar(e_buf[:, b, t, :], e_buf[:, b, t, :], erec[:, 2 * h + 1, t:t + 1], None, ALU.mult
                                    ).then_inc(comb_tmp, 1)
                for t in range(TT):
                    dve.wait_ge(comb_tmp, 2 * h + t + 1)
                    V.scalar_tensor_tensor(e_buf[:, a, t, :], e_buf[:, a, t, :], erec[:, 2 * h, t:t + 1],
                                           e_buf[:, b, t, :], ALU.mult, ALU.add).then_inc(comb_done, 1)

            dve.wait_ge(lam_done, 2)
            V.tensor_tensor(lam[:, 0:1], lam[:, 3:4], lam[:, 2:3], ALU.subtract).then_inc(lam_done, 1)
            dve.wait_ge(lam_done, 3)
            V.tensor_scalar(lam[:, 0:1], lam[:, 0:1], -LAM0, None, ALU.add).then_inc(lam_done, 1)
            dve.wait_ge(lam_done, 4)
            n0 = 2 * WIN_PAIR
            for w in range(12):
                split_lo(n0 + w + 1)
                if w < 4:
                    g = 7 + w // 2
                    for j in range(4 * (w % 2), 4 * (w % 2) + 4):
                        ada_tile(g, j, gates=1)
                    if w % 2:
                        mod_out(g)
                if w in (4, 5):
                    qk_norm(w - 4, 0, RS_AT[1] + 2 + (w - 4) + 1)
                if w >= 6:
                    h = w - 6
                    if 1 <= h <= 4:
                        combine(h - 1)
                    if h < 4:
                        row_max(2 * h)
                        row_max(2 * h + 1)
                if w == 10:
                    qk_norm(0, 1, RS_AT[1] + 2 + 3)
                if w == 11:
                    qk_norm(1, 1, RS_AT[1] + 2 + 4)
            split_lo(n0 + 13)
            diag(GATES[1], 1, 1.0)

            def a_output(t):
                dve.wait_ge(osq_done, t + 1)
                V.tensor_reduce(ss[:, 4 * t:4 * t + 4], mix[:, t, 0:512].rearrange("p (h d) -> p h d", d=P), AX.X,
                                ALU.add).then_inc(ored_done, 1)

            def a_scale(t):
                dve.wait_ge(rstd_done, RS_AT[1] + 2 + 4 + t + 1)
                m = mix[:, t, 0:512].rearrange("p (h d) -> p h d", d=P)
                V.tensor_tensor(m, ps[:, 2 + t, :].rearrange("p (h d) -> p h d", d=P),
                                rstd[:, 4 * t:4 * t + 4].unsqueeze(2).to_broadcast([P, 4, P]), ALU.mult
                                ).then_inc(omul_done, 1)
                dve.wait_ge(omul_done, t + 1)
                V.tensor_tensor(m, m, subln[:, :].unsqueeze(1).to_broadcast([P, 4, P]), ALU.mult
                                ).then_inc(mix_done, 1)

            a_output(0)
            a_output(1)
            a_scale(0)
            a_scale(1)
            for b in range(B_HEADS):
                row_max(8 + b)
            dve.wait_ge(exp_done, 32)
            V.reciprocal(erec[:, 8:16, :], esum[:, 8:16, :]).then_inc(erec_done, 1)
            dve.wait_ge(erec_done, 2 * A_HEADS + 1)
            dve.wait_ge(pv_done, A_HEADS + B_HEADS)
            for t in range(TT):
                V.tensor_tensor(mix[:, t, 512:1024].rearrange("p (h d) -> p h d", d=HD),
                                ps[:, 2 + t, :].rearrange("p (h d) -> p h d", d=HD),
                                erec[:, 8:16, t:t + 1].to_broadcast([P, 8, HD]), ALU.mult).then_inc(mix_done, 1)
            for j2 in range(4):
                n = TP_MIX + j2
                dve.wait_ge(tp_out, n + 1)
                split_h(j2)
            for n in (36, 37, 38):
                split_lo(n)
            make_acol(2)
            residual(2, 1, unit_used, 2 * WOUT_PAIR + 4)
            norm(2)
            ffn(1, m0=9, turns=5, gates=2)
            make_acol(3)
            residual(3, 2, w2_used, w2_count(2 * NC - 1), y0=2)
            norm(3, 2 * FFN_PAIR[2])
            ffn(2, m0=14, turns=4, gates=3)
            make_acol(4)
            residual(4, 3, w2_used, w2_count(3 * NC - 1), y0=3)
            split_lo(2 * POOL_PAIR)
            norm_scale(4)

            diag(GATES[4], 4, 1.0)
            split_lo(83)
            step = [0]

            dve.wait_ge(acol_done, 5)

            def pool_low(g):
                dve.wait_ge(pooled_hi, g + 1)
                V.tensor_tensor(hT_lo[:, 2 * g:2 * g + 2, :], pool_y(arena, g),
                                hT_hi[:, 2 * g:2 * g + 2, :].bitcast(F32), ALU.subtract).then_inc(hlo_done, 2)

            def link(ins):
                step[0] += 1
                ins.then_inc(pool_step, 1)
                dve.wait_ge(pool_step, step[0])

            hp = hpad(arena)
            link(V.memset(hp[:, :, 0:8], 0.0))
            link(V.memset(hp[:, :, 8 + SEQ:16 + SEQ], 0.0))
            gsh = NMOD + 3
            for j in range(KT):
                dve.wait_ge(xT_done, 4 * 4 + j // 2 + 1)
                link(V.tensor_scalar(hp[:, j, 8:8 + SEQ],
                                     ps[:, norm_bank(4, j), (j % 2) * 256:(j % 2) * 256 + 256],
                                     acol[:, 4, j:j + 1], modc[:, gsh, j:j + 1], ALU.mult, ALU.add))
            dve.wait_ge(pool_in, 48)
            for g, win in enumerate(WINDOWS):
                cur = hp[:, 2 * g:2 * g + 2, :]
                width = SEQ + 16
                span = 1
                bufs = pool_tmp(arena)
                k = 0
                off = 0
                while span < win:
                    width -= span
                    nxt = bufs[k % 2][:, :, 0:width]
                    link(V.tensor_tensor(nxt, cur[:, :, 0:width], cur[:, :, span:span + width], ALU.add))
                    cur, span, k = nxt, 2 * span, k + 1
                start = 8 - win // 2
                y = pool_y(arena, g)
                cnt = mix[:, 0, g * SEQ:(g + 1) * SEQ].unsqueeze(1).to_broadcast([P, 2, SEQ])
                link(V.tensor_tensor(y, cur[:, :, start:start + SEQ], cnt, ALU.mult))
                link(V.tensor_tensor(y, y, hp[:, 2 * g:2 * g + 2, 8:8 + SEQ], ALU.subtract))
                assert step[0] == POOL_STEPS[g]
                if g >= 1:
                    pool_low(g - 1)
            pool_low(3)
            split_lo(84)
            dve.wait_ge(gate_ready, 5)
            link(V.tensor_tensor(gate[:, :], gate[:, :], v_sb[:, 1, :], ALU.mult))
            link(V.tensor_tensor(v_sb[:, 0, :], v_sb[:, 0, :], gate[:, :], ALU.mult))
            for t in range(TT):
                link(V.tensor_tensor(x[:, t, :], x[:, t, :], v_sb[:, 0, :], ALU.add))
            make_acol(5)
            residual(5, 4, unit_used, 2 * POOL_PAIR + 2)
            norm(5)
            ffn(3)
            residual(6, 5, w2_used, w2_count(4 * NC - 1), y0=4)

        @block.tensor
        def _(pe):
            mm = nc.tensor.matmul

            def norm(s):
                for t in range(TT):
                    pe.wait_ge(xn_done, 2 * s + t + 1)
                    for j in range(KT):
                        c0 = (j % 2) * 256 + t * P
                        ins = nc.tensor.transpose(ps[:, norm_bank(s, j), c0:c0 + P], xn[:, t, j * P:(j + 1) * P],
                                                  ident[:, :])
                        if t == TT - 1 and j % 2:
                            ins.then_inc(xT_done, 1)

            def three(out, pairs, first, last):
                for m, (a, b) in enumerate(pairs):
                    ins = mm(out, a, b, start=first and m == 0, stop=last and m == len(pairs) - 1)
                return ins

            def w13(s, Q, n, i4=0, hs=None):
                pe.wait_ge(lo13_done, i4 + (n + 1))
                for ab in range(2):
                    for k in range(KT):
                        if hs is not None and ab == 0:
                            pe.wait_ge(hlo_done, hs + k + 1)
                        w0 = (ab * KT + k) * P
                        wh, wl = hi13[:, n % 2, w0:w0 + P], lo13[:, n % 2, w0:w0 + P]
                        hh, hl = hT_hi[:, k, :], hT_lo[:, k, :]
                        ins = three(ps[:, 4 + Q % 2, ab * 256:ab * 256 + 256], ((wh, hh), (wh, hl), (wl, hh)),
                                    k == 0, k == KT - 1)
                ins.then_inc(unit_used, 1)

            def w2(Q, i4=0, tiles=range(TT), last=False, done=w2_used):
                pe.wait_ge(ulo_done, i4 + (Q + 1))
                pe.wait_ge(lo2_done, i4 + (Q + 1))
                p = Q % 2
                for t in tiles:
                    uh, ul = u_hi[:, p, t * P:(t + 1) * P], u_lo[:, p, t * P:(t + 1) * P]
                    for h in range(2):
                        wh, wl = hi2[:, p, h * 512:h * 512 + 512], lo2[:, p, h * 512:h * 512 + 512]
                        mm(ps[:, 2 * t + h, :], uh, wh, start=False, stop=False)
                        mm(ps[:, 2 * t + h, :], uh, wl, start=False, stop=False)
                    for h in range(2):
                        wh = hi2[:, p, h * 512:h * 512 + 512]
                        ins = mm(ps[:, 2 * t + h, :], ul, wh, start=False, stop=last)
                if done is not None:
                    ins.then_inc(done, 1)

            def mod_sum(g, i=0):
                pe.wait_ge(ada_used, KT * i + KT * (g + 1))
                if g >= 1:
                    pe.wait_ge(mod_done, i + g)
                for j in range(KT):
                    c0 = (j % 4) * P
                    ins = nc.tensor.transpose(ps[:, MOD_BANK + j // 4, c0:c0 + P], acc[:, j * P:(j + 1) * P],
                                              ident[:, :])
                ins.then_inc(mod_ps, 1)

            def gate_row(k, mods):
                pe.wait_ge(diag_done, KT * (k + 1))
                pe.wait_ge(mod_done, mods)
                for h in range(2):
                    ins = mm(ps[:, 6 + h, :], ones[:, :], acc[:, h * 512:h * 512 + 512], start=True, stop=True)
                ins.then_inc(gate_ps, 1)

            def ffn(f, m0=None, turns=0, mods=0):
                s = SUB_OF_FFN[f]
                Q0, n0 = NC * f, 2 * FFN_PAIR[f]
                w13(s, Q0, n0, hs=HLO[s])
                for b in range(4):
                    ins = mm(ps[:, b, :], zeros[:, :], zeros[:, 0:1].to_broadcast([P, 512]), start=True, stop=False)
                ins.then_inc(w2_used, 1)

                def body(i, with_mod):
                    i4 = 4 * i
                    for d in range(4):
                        Q = Q0 + 1 + d
                        w13(s, Q, n0 + 1 + d, i4)
                        if with_mod and d == 3:
                            mod_sum(m0, i)
                        w2(Q - 1, i4)

                if turns:
                    with pe.Fori(0, turns) as i:
                        body(i, True)
                if turns == 0:
                    with pe.Fori(0, 5) as i:
                        body(i, False)
                elif turns < 5:
                    body(turns, False)
                w13(s, Q0 + 21, n0 + 21)
                w2(Q0 + 20, tiles=[0], done=None)
                gate_row(s, mods)
                w2(Q0 + 21, tiles=[0], last=True, done=y0_done)
                w2(Q0 + 20, tiles=[1])
                w2(Q0 + 21, tiles=[1], last=True)

            pe.wait_ge(setup_done, 2)
            pe.wait_ge(ident_in, 16)
            norm(0)
            mod_sum(0)
            mod_sum(1)
            ffn(0, m0=2, turns=5, mods=7)
            norm(1)

            def proj(n, hs=None, out_of=None):
                pe.wait_ge(lo13_done, n + 1)
                for t in range(TT):
                    for k in range(KT):
                        if hs is not None and t == 0:
                            pe.wait_ge(hlo_done, hs + k + 1)
                        tok = slice(t * P, (t + 1) * P)
                        hh, hl = hT_hi[:, k, tok], hT_lo[:, k, tok]
                        wh, wl = hi13[:, n % 2, k * 256:k * 256 + 256], lo13[:, n % 2, k * 256:k * 256 + 256]
                        ins = three(out_of(t), ((hh, wh), (hh, wl), (hl, wh)), k == 0, k == KT - 1)
                ins.then_inc(unit_used, 1)

            tp = [0]

            def tp_bank():
                n = tp[0]
                if n >= 2:
                    pe.wait_ge(tp_out, n - 1)
                tp[0] += 1
                return n % 2

            def qk_transpose(ab):
                pe.wait_ge(qk_done, 4 * ab + 4)
                for b2 in range(4):
                    bank = tp_bank()
                    for b in range(2):
                        for t in range(TT):
                            blk = 2 * b2 + b
                            ins = nc.tensor.transpose(ps[:, bank, b * 256 + t * P:b * 256 + t * P + P],
                                                      xn[:, t, blk * P:(blk + 1) * P], ident[:, :])
                    ins.then_inc(tp_fill, 1)

            def scores(u, tp_need):
                pe.wait_ge(tp_out, tp_need)
                if u >= 2:
                    pe.wait_ge(exp_done, 2 * (u - 1))
                v = u % (2 * A_HEADS)
                rows = slice((v % 2) * 64, (v % 2) * 64 + 64)
                for t in range(TT):
                    ins = mm(ps[:, 6 + u % 2, t * 256:t * 256 + 256], qkT[rows, v // 2, t * P:(t + 1) * P],
                             qkT[rows, 4 + v // 2, :], start=True, stop=u < 2 * A_HEADS)
                    if u >= 2 * A_HEADS:
                        ins = mm(ps[:, 6 + u % 2, t * 256:t * 256 + 256], exch[:, :],
                                 bias[:, t, v, :, :].rearrange("p r c -> p (r c)"), start=False, stop=True)
                ins.then_inc(score_done, 1)

            def weights_transpose(k):
                bank = tp_bank()
                if k < A_HEADS:
                    pe.wait_ge(comb_done, 2 * (k + 1))
                    slot = (2 * k) % 4
                else:
                    u = 2 * A_HEADS + k - A_HEADS
                    pe.wait_ge(exp_done, 2 * (u + 1))
                    slot = u % 4
                for kt in range(2):
                    for t in range(TT):
                        ins = nc.tensor.transpose(ps[:, bank, kt * 256 + t * P:kt * 256 + t * P + P],
                                                  e_buf[:, slot, t, kt * P:(kt + 1) * P], ident[:, :])
                ins.then_inc(tp_fill, 1)

            def values(k):
                pe.wait_ge(tp_out, TP_HEAD(k) + 1)
                if k == 0:
                    pe.wait_ge(win_out, 6)
                if k == A_HEADS:
                    pe.wait_ge(win_out, 12)
                    pe.wait_ge(mix_done, 2)
                for t in range(TT):
                    for kt in range(2):
                        if k < A_HEADS:
                            dst, v = ps[:, 2 + t, k * P:(k + 1) * P], v_sb[:, kt, k * P:(k + 1) * P]
                        else:
                            b = k - A_HEADS
                            dst, v = ps[:, 2 + t, b * HD:(b + 1) * HD], v_sb[:, kt, 512 + b * HD:512 + (b + 1) * HD]
                        ins = mm(dst, ptT[k % 2][:, kt, t * P:(t + 1) * P], v, start=kt == 0, stop=kt == 1)
                ins.then_inc(pv_done, 1)

            n0 = 2 * WIN_PAIR
            for w in range(12):
                if w >= 2:
                    pe.wait_ge(win_out, w - 1)
                if w == 6:
                    qk_transpose(0)
                proj(n0 + w, hs=HLO[1] if w == 0 else None,
                     out_of=lambda t, w=w: ps[:, 4 + w % 2, t * 256:t * 256 + 256])
                if w == 1:
                    mod_sum(7)
                if w == 3:
                    mod_sum(8)
                if w == 4:
                    pe.wait_ge(mod_done, 9)
                if w >= 6:
                    h = w - 6
                    if h < 4:
                        scores(2 * h, 4)
                        scores(2 * h + 1, 4)
                    if 1 <= h <= 4:
                        weights_transpose(h - 1)
                    if 2 <= h <= 5:
                        values(h - 2)
            qk_transpose(1)
            pe.wait_ge(bias_done, 8)
            for b in range(B_HEADS + 2):
                if b < B_HEADS:
                    scores(8 + b, 12)
                if 1 <= b <= B_HEADS:
                    weights_transpose(3 + b)
                if b >= 2:
                    values(2 + b)
            pe.wait_ge(exp_done, 2 * (2 * A_HEADS + B_HEADS))
            gate_row(1, 9)
            pe.wait_ge(mix_done, 4)
            for j2 in range(4):
                bank = tp_bank()
                for jj in range(2):
                    for t in range(TT):
                        j = 2 * j2 + jj
                        ins = nc.tensor.transpose(ps[:, bank, jj * 256 + t * P:jj * 256 + t * P + P],
                                                  mix[:, t, j * P:(j + 1) * P], ident[:, :])
                ins.then_inc(tp_fill, 1)
            pe.wait_ge(hlo_done, HLO[1] + 16)
            for v in range(4):
                proj(2 * WOUT_PAIR + v, out_of=lambda t, v=v: ps[:, 2 * t + v // 2, (v % 2) * 256:(v % 2) * 256 + 256])
            norm(2)
            ffn(1, m0=9, turns=5, mods=14)
            norm(3)
            ffn(2, m0=14, turns=4, mods=18)
            norm(4)

            for g in range(4):
                n = 2 * POOL_PAIR + g // 2
                pe.wait_ge(lo13_done, n + 1)
                pe.wait_ge(hlo_done, HLO[4] + 2 * g + 2)
                if g == 0:
                    pe.wait_ge(pool_step, 2 + KT)
                for t in range(TT):
                    for kk in range(2):
                        k = 2 * g + kk
                        tok = slice(t * P, (t + 1) * P)
                        c0 = ((2 * g + kk) % 4) * 256
                        hh, hl = hT_hi[:, k, tok], hT_lo[:, k, tok]
                        wh, wl = hi13[:, n % 2, c0:c0 + 256], lo13[:, n % 2, c0:c0 + 256]
                        dst = ps[:, 2 * t + g // 2, (g % 2) * 256:(g % 2) * 256 + 256]
                        ins = three(dst, ((hh, wh), (hh, wl), (hl, wh)), kk == 0, kk == 1)
                if g % 2:
                    ins.then_inc(unit_used, 1)
            gate_row(4, 18)
            norm(5)
            ffn(3, mods=18)


def kernel(**inputs):
    import concourse.bacc as bacc
    from concourse.bass_utils import run_bass_kernel_spmd

    a = {k: np.ascontiguousarray(v) for k, v in inputs.items()}
    a["c"] = np.ascontiguousarray(a["c"].reshape(KT, P).T)
    a["ada_b"] = np.ascontiguousarray(a["ada_b"].reshape(2 * NMOD, KT, P).transpose(2, 0, 1))
    a["norm_g"] = np.ascontiguousarray(a["norm_g"].reshape(6, KT, P).transpose(2, 0, 1))
    inv = np.float32(10000.0) ** (-np.arange(0, HD, 2, dtype=np.float32) / np.float32(HD))
    ang = np.arange(SEQ, dtype=np.float32)[:, None] * inv[None, :]
    table = np.stack([np.cos(ang), np.sin(ang)]).astype(np.float32)
    a["rope_cs"] = np.ascontiguousarray(table.reshape(2, TT, P, HD // 2).transpose(2, 0, 1, 3))
    t = np.arange(SEQ)
    counts = [np.clip(t - w // 2 + w, 0, SEQ) - np.clip(t - w // 2, 0, SEQ) for w in WINDOWS]
    a["inv_count"] = (1.0 / np.stack(counts)).astype(np.float32)
    a["identity"] = np.eye(P, dtype=np.float32)
    a["exchange"] = np.ascontiguousarray(a["identity"].reshape(P, 2, P // 2)[:, :, ::-1].reshape(P, P))

    nc = bacc.Bacc("TRN2", target_bir_lowering=False, num_devices=1)
    order = ["x", "c", "ada_w", "ada_b", "norm_g", "ff_w13", "ff_w2", "w_in", "w_out", "a_qk_norm",
             "a_lambda", "a_subln", "b_qk_norm", "b_rpb", "pool_w", "pool_b", "pool_scale",
             "rope_cs", "inv_count", "identity", "exchange"]
    arrays, args = {}, []
    for name in order:
        arrays[f"in_{name}"] = a[name]
        args.append(nc.dram_tensor(f"in_{name}", a[name].shape, mybir.dt.from_np(a[name].dtype),
                                   kind="ExternalInput").ap())
    out = nc.dram_tensor("out_dram", (1, SEQ, D), F32, kind="ExternalOutput").ap()
    build_program(nc, *args, out)
    r = run_bass_kernel_spmd(nc, [arrays], core_ids=[0])
    return r.results[0]["out_dram"]
```

```python
import math
from contextlib import ExitStack

import numpy as np

import concourse.bass as bass
from concourse import mybir

P = 128
D = 1024
SEQ = 256
TT = SEQ // P
KT = D // P
DFF = 2816
NC = DFF // P
NMOD = 9
HD = 64
A_HEADS = 4
B_HEADS = 8
GRID_W = 64
ROWS = SEQ // GRID_W
NA_ROWS, NA_COLS = 8, 16
EPS = 1e-6
NEG = -1e30
LAM0 = 0.8 - 0.6 * math.exp(0.0)
SCALE = HD ** -0.5
WINDOWS = (2, 4, 8, 16)

F32 = mybir.dt.float32
F32R = mybir.dt.float32r
BF16 = mybir.dt.bfloat16
ACT = mybir.ActivationFunctionType
ALU = mybir.AluOpType
AX = mybir.AxisListType

FFN_PAIR = [0, 19, 30, 42]
WIN_PAIR, WOUT_PAIR, POOL_PAIR = 11, 17, 41
ADA_RING = 4
SUB_OF_FFN = [0, 2, 3, 5]
GATES = [NMOD * (s // 3) + 3 * (s % 3) + 2 for s in range(6)]
MOD_BANK = 6
H32 = [0, 8, 16, 24, 32, 40]
HLO = [0, 8, 24, 32, 40, 48]
RS_AT = [0, 2, 9, 11, 13, 15]
POOL_BANK = [2, 3, 6, 7]
WIN_SEGS = [(seg, half) for seg in ("qa", "ka", "va", "qb", "kb", "vb") for half in range(2)]
TP_MIX = 16


def norm_bank(s, j):
    return ([5, 0, 1, 2] if s == 0 else [5, 0, 1, 4] if s == 4 else [5, 6, 0, 1])[j // 2]


def TP_HEAD(k):
    return 4 + k if k < A_HEADS else 8 + k if k < A_HEADS + 4 else 10 + k


def slot_free(u):
    before = u - 4
    head = before // 2 if before < 2 * A_HEADS else before - 2 * A_HEADS + A_HEADS
    return TP_HEAD(head) + 1


def w2_count(Q):
    return Q + Q // NC + 2


def row_bcast(src, n):
    return bass.AP(tensor=src.tensor, offset=src.offset, ap=[[0, P], [1, n]])


def build_program(nc, x_in, c_col, ada_w, ada_bT, norm_gT, ff_w13, ff_w2, w_in, w_out, a_qk_norm,
                  a_lambda, a_subln, b_qk_normT, b_rpb, pool_w, pool_b, pool_scale,
                  rope_cs, pool_avg, identity, exchange, out):
    ctx = ExitStack()
    with ctx:
        def sb(name, shape, dt=F32):
            return ctx.enter_context(nc.sbuf_tensor(name, shape, dt))

        def sem(name):
            return ctx.enter_context(nc.semaphore(name))

        raw13 = sb("raw13", [P, 2, 2, KT, 256])
        raw2 = sb("raw2", [P, 2, D])
        hi13 = sb("hi13", [P, 2, 2048], F32R)
        lo13 = sb("lo13", [P, 2, 2048], F32R)
        hi2 = sb("hi2", [P, 2, D], F32R)
        lo2 = sb("lo2", [P, 2, D], F32R)
        ada = sb("ada", [P, ADA_RING, D])
        acc = sb("acc", [P, D])
        x = sb("x", [P, TT, D])
        xn = sb("xn", [P, TT, D])
        hT_hi = sb("hT_hi", [P, KT, SEQ], F32R)
        hT_lo = sb("hT_lo", [P, KT, SEQ], F32R)
        gate = sb("gate", [P, D])
        s_buf = sb("s_buf", [P, 2, SEQ])
        u_buf = sb("u_buf", [P, 2, SEQ])
        u_hi = sb("u_hi", [P, 2, SEQ], F32R)
        u_lo = sb("u_lo", [P, 2, SEQ], F32R)
        arena = sb("arena", [P, 12288])
        bias = arena[:, 0:4096].rearrange("p (t h r c) -> p t h r c", t=TT, h=B_HEADS, r=ROWS)
        qkT = arena[:, 4096:6144].rearrange("p (b n) -> p b n", b=8)
        h32 = qkT
        v_sb = arena[:, 6144:8192].rearrange("p (t n) -> p t n", t=TT)
        mix = arena[:, 8192:10240].rearrange("p (t n) -> p t n", t=TT)
        pooled = arena[:, 0:2048].rearrange("p (j n) -> p j n", j=KT)
        avg = arena[:, 2048:4096].rearrange("p (w t n) -> p w t n", w=4, t=TT)
        pool_gate = mix[:, 0, :]
        e_buf = arena[:, 10240:12288].rearrange("p (s t n) -> p s t n", s=4, t=TT)
        modc = sb("modc", [P, 2 * NMOD, KT])
        mraw = sb("mraw", [P, 1, KT])
        adab = sb("adab", [P, 2 * NMOD, KT])
        ngT = sb("ngT", [P, 6, KT])
        acol = sb("acol", [P, 6, KT])
        cond = sb("cond", [P, KT])
        ident = sb("ident", [P, P])
        ones = sb("ones", [P, P])
        zeros = sb("zeros", [P, P], BF16)
        exch = sb("exch", [P, P])
        neg_half = sb("neg_half", [P, 32])
        ss = sb("ss", [P, 32])
        rstd = sb("rstd", [P, 32])
        gnorm = sb("gnorm", [P, 2, HD])
        bnorm = sb("bnorm", [P, 2])
        rope = arena[:, 10240:10368].rearrange("p (c t d) -> p c t d", c=2, t=TT)
        lamb = arena[:, 10368:10624].rearrange("p (a d) -> p a d", a=4)
        subln = sb("subln", [P, P])
        lam = sb("lam", [P, 4])
        nmx = sb("nmx", [P, 16, TT])
        esum = sb("esum", [P, 16, TT])
        erec = sb("erec", [P, 16, TT])
        rope_g = sb("rope_g", [P, 2, TT, 2, HD])
        ps = ctx.enter_context(nc.psum_tensor("ps", [P, 8, 512], F32))

        first_ada = [raw13[:, 1, m, :, :].rearrange("p (a k) n -> p a (k n)", a=2) for m in range(2)]
        first_ada += [arena[:, c:c + 2 * D].rearrange("p (a n) -> p a n", a=2) for c in (0, 2 * D, 6 * D, 8 * D)]

        ptT = [s_buf, u_buf]

        raw13_in = [sem(f"raw13_in{i}") for i in range(2)]
        raw2_in = [sem(f"raw2_in{i}") for i in range(2)]
        first_in = [sem(f"first_in{i}") for i in range(6)]
        ada_in = [sem(f"ada_in{i}") for i in range(ADA_RING)]
        hi13_done, lo13_done, unit_used = sem("hi13_done"), sem("lo13_done"), sem("unit_used")
        hi2_done, lo2_done, w2_used = sem("hi2_done"), sem("lo2_done"), sem("w2_used")
        y0_done = sem("y0_done")
        silu_done, u_done = sem("silu_done"), sem("u_done")
        uhi_done, ulo_done = sem("uhi_done"), sem("ulo_done")
        ada_used, mod_ps, mod_red, mod_done = sem("ada_used"), sem("mod_ps"), sem("mod_red"), sem("mod_done")
        diag_done, gate_ps, gate_ready = sem("diag_done"), sem("gate_ps"), sem("gate_ready")
        x_tmp, x_done = sem("x_tmp"), sem("x_done")
        ss_done, rstd_tmp, rstd_done, xn_done = sem("ss_done"), sem("rstd_tmp"), sem("rstd_done"), sem("xn_done")
        xT_done, acol_done = sem("xT_done"), sem("acol_done")
        h32_done, hhi_done, hlo_done = sem("h32_done"), sem("hhi_done"), sem("hlo_done")
        ident_in, adab_in = sem("ident_in"), sem("adab_in")
        small_in, x_in_sem, cond_done = sem("small_in"), sem("x_in_sem"), sem("cond_done")
        setup_done, half_set, bias_in, bias_done = sem("setup_done"), sem("half_set"), sem("bias_in"), sem("bias_done")
        lam_done, setup_step = sem("lam_done"), sem("setup_step")
        win_out = sem("win_out")
        sq_done, qred_done, qk_step, qk_done = sem("sq_done"), sem("qred_done"), sem("qk_step"), sem("qk_done")
        tp_fill, tp_out = sem("tp_fill"), sem("tp_out")
        score_done, nmx_tmp, nmx_done, exp_done = sem("score_done"), sem("nmx_tmp"), sem("nmx_done"), sem("exp_done")
        bnorm_done, en_done, mixb_hi = sem("bnorm_done"), sem("en_done"), sem("mixb_hi")
        erec_done, comb_tmp, comb_done, pv_done = sem("erec_done"), sem("comb_tmp"), sem("comb_done"), sem("pv_done")
        osq_done, ored_done, omul_done, mix_done = sem("osq_done"), sem("ored_done"), sem("omul_done"), sem("mix_done")
        pool_in, avg_in, pool_step = sem("pool_in"), sem("avg_in"), sem("pool_step")
        pool_ps, pooled_done, diff_done = sem("pool_ps"), sem("pooled_done"), sem("diff_done")
        out_sem = sem("out_sem")

        def raw13_count(pair):
            return 32 * (pair // 2 + 1)

        w13_v = [ff_w13[f // 2, f % 2].rearrange("(k p) n -> p k n", p=P) for f in range(4)]
        w2_v = [ff_w2[f // 2, f % 2].rearrange("(c p) n -> p c n", p=P) for f in range(4)]
        win_v = w_in[0].rearrange("(k p) n -> p k n", p=P)
        wout_v = w_out[0].rearrange("(k p) n -> p k n", p=P)
        pw_v = pool_w[0].rearrange("g (k p) n -> p (g k) n", p=P)
        ada_v = [ada_w[l].rearrange("(j p) n -> p j n", p=P) for l in range(2)]
        out_v = out[0].rearrange("(t p) n -> p t n", p=P)
        x_v = x_in[0].rearrange("(t p) n -> p t n", p=P)

        def unit_src(n):
            pair, half = n // 2, n % 2
            slot = pair % 2
            for f in range(4):
                if FFN_PAIR[f] <= pair < FFN_PAIR[f] + 11:
                    src = raw13[:, slot, :, :, half * P:half * P + P].rearrange("p h k n -> p (h k) n")
                    return src, [t[:, half, :].rearrange("p (a n) -> p a n", n=P) for t in (hi13, lo13)]
            if pair == POOL_PAIR:
                return (raw13[:, slot, half, 0:4, :].rearrange("p k n -> p (k n)"),
                        [t[:, half, 0:1024] for t in (hi13, lo13)])
            return (raw13[:, slot, half, :, :].rearrange("p k n -> p (k n)"),
                    [t[:, half, :] for t in (hi13, lo13)])

        block = ctx.enter_context(nc.Block())

        @block.sync
        def _(sp):
            def free13(pair):
                if pair >= 2:
                    sp.wait_ge(lo13_done, 2 * (pair - 2) + 2)

            def load_pair(pair, srcs):
                free13(pair)
                for h in range(2):
                    dst = raw13[:, pair % 2, h, 0:srcs[h].shape[1], :]
                    sp.dma_start(dst, srcs[h]).then_inc(raw13_in[pair % 2], 16)

            def load_w2(f, q):
                n = NC * f + q
                if n >= 2:
                    sp.wait_ge(lo2_done, n - 1)
                sp.dma_start(raw2[:, n % 2, :], w2_v[f][:, q, :]).then_inc(raw2_in[n % 2], 16)

            sp.dma_start(ident[:, :], identity).then_inc(ident_in, 16)
            sp.dma_start(x[:, 0, :], x_v[:, 0, :]).then_inc(x_in_sem, 16)
            sp.dma_start(x[:, 1, :], x_v[:, 1, :]).then_inc(x_in_sem, 16)
            for m in range(6):
                g, j = (4 + 2 * m) // KT, (4 + 2 * m) % KT
                if m == 2:
                    load_pair(0, [w13_v[0][:, :, h * DFF:h * DFF + 256] for h in range(2)])
                sp.dma_start(first_ada[m], ada_v[0][:, j:j + 2, g * D:(g + 1) * D]).then_inc(first_in[m], 16)
            for f in range(4):
                base = FFN_PAIR[f]
                for e in range(2):
                    if f == 0 and e == 0:
                        continue
                    if f == 0 and e == 1:
                        sp.wait_ge(ada_used, 2 * KT - 4)
                        load_w2(0, 0)
                    load_pair(base + e, [w13_v[f][:, :, h * DFF + e * 256:h * DFF + e * 256 + 256]
                                         for h in range(2)])
                    if f > 0 or e == 1:
                        load_w2(f, e)

                def turn(i):
                    for e in range(2):
                        pair = base + 2 + e
                        sp.wait_ge(lo13_done, 4 * i + (2 * pair - 2))
                        for h in range(2):
                            sp.dma_start(raw13[:, pair % 2, h, :, :],
                                         w13_v[f][:, :, bass.ds(i * 512 + (h * DFF + (2 + e) * 256), 256)]
                                         ).then_inc(raw13_in[pair % 2], 16)
                        for g in range(2):
                            load_w2_turn(i, 2 + 2 * e + g)

                def load_w2_turn(i, q):
                    n = NC * f + q
                    sp.wait_ge(lo2_done, 4 * i + (n - 1))
                    sp.dma_start(raw2[:, n % 2, :],
                                 w2_v[f][:, bass.ds(4 * i + q, 1), :].rearrange("p a n -> p (a n)")
                                 ).then_inc(raw2_in[n % 2], 16)

                with sp.Fori(0, 4) as i:
                    turn(i)
                load_pair(base + 10, [w13_v[f][:, :, h * DFF + 2560:h * DFF + 2816] for h in range(2)])
                for q in range(18, NC):
                    load_w2(f, q)
                if f == 0:
                    for t in range(TT):
                        for half in range(2):
                            rq = 2 * t + half
                            for rk in range(ROWS):
                                off = (rk - rq + NA_ROWS - 1) * (2 * NA_COLS - 1) + NA_COLS - GRID_W
                                src = bass.AP(tensor=b_rpb.tensor, offset=off,
                                              ap=[[1, 64], [(2 * NA_ROWS - 1) * (2 * NA_COLS - 1), B_HEADS], [1, GRID_W]])
                                sp.dma_start(bias[half * 64:half * 64 + 64, t, :, rk, :], src).then_inc(bias_in, 16)
                    for w in range(6):
                        load_pair(WIN_PAIR + w, [win_v[:, :, c:c + 256] for c in (512 * w, 512 * w + 256)])
                    for w in range(2):
                        load_pair(WOUT_PAIR + w, [wout_v[:, :, w * 512 + h * 256:w * 512 + h * 256 + 256]
                                                  for h in range(2)])
                if f == 2:
                    load_pair(POOL_PAIR, [pw_v[:, 4 * h:4 * h + 4, :] for h in range(2)])
            for t in range(TT):
                sp.wait_ge(x_done, 2 * 5 + t + 1)
                sp.dma_start(out_v[:, t, :], x[:, t, :]).then_inc(out_sem, 16)
            sp.wait_ge(out_sem, 32)

        @block.gpsimd
        def _(pool):
            def ada_vector(g, first=0, last=KT):
                for j in range(first, last):
                    n = KT * g + j
                    if g > 0:
                        pool.wait_ge(ada_used, n - ADA_RING + 1)
                    pool.dma_start(ada[:, j % ADA_RING, :], ada_v[0][:, j, g * D:(g + 1) * D]
                                   ).then_inc(ada_in[j % ADA_RING], 16)

            ada_vector(0, 0, ADA_RING)
            nc.gpsimd.memset(neg_half[:, :], -0.5).then_inc(half_set, 1)
            def rms(width, wait_sem, wait_at, cols, tmp_at):
                pool.wait_ge(wait_sem, wait_at)
                nc.gpsimd.tensor_scalar(rstd[:, cols], ss[:, cols], 1.0 / width, EPS, ALU.mult, ALU.add
                                        ).then_inc(rstd_tmp, 1)
                pool.wait_ge(rstd_tmp, tmp_at)
                nc.gpsimd.tensor_tensor(rstd[:, cols], rstd[:, cols], neg_half[:, cols], ALU.pow
                                        ).then_inc(rstd_done, 1)

            rms_n = [0]

            def next_rms(width, wait_sem, wait_at, cols):
                rms_n[0] += 1
                rms(width, wait_sem, wait_at, cols, rms_n[0])

            pool.wait_ge(half_set, 1)
            for t in range(TT):
                next_rms(D, ss_done, t + 1, slice(t, t + 1))
            def ada_loop(layer, m0, done, turns):
                with pool.Fori(0, turns) as i:
                    for j in range(KT):
                        pool.wait_ge(ada_used, KT * i + (KT * done + j - ADA_RING + 1))
                        pool.dma_start(ada[:, j % ADA_RING, :],
                                       ada_v[layer][:, j, bass.ds(i * D + m0 * D, D)]
                                       ).then_inc(ada_in[j % ADA_RING], 16)

            def norm_rms(s):
                for t in range(TT):
                    next_rms(D, ss_done, 2 * s + t + 1, slice(t, t + 1))

            ada_loop(0, 2, 2, 5)
            norm_rms(1)
            ada_vector(7)
            pool.wait_ge(bias_in, 16 * TT * 2 * ROWS)
            step = [0]
            for t in range(TT):
                for half in range(2):
                    rows = slice(half * 64, half * 64 + 64)
                    low = bias[rows, t, :, :, 0:48].rearrange("p h r c -> p (h r) c")
                    high = bias[rows, t, :, :, 16:64].rearrange("p h r c -> p (h r) c")
                    nc.gpsimd.affine_select(out=low, in_=low, compare_op=ALU.is_ge, fill=NEG,
                                            base=NA_COLS // 2 - (GRID_W - 1),
                                            pattern=[[0, 32], [1, 48]], channel_multiplier=1).then_inc(bias_done, 1)
                    step[0] += 1
                    pool.wait_ge(bias_done, step[0])
                    nc.gpsimd.affine_select(out=high, in_=high, compare_op=ALU.is_ge, fill=NEG,
                                            base=NA_COLS // 2 - 1 - NA_COLS + (GRID_W - 1),
                                            pattern=[[0, 32], [-1, 48]], channel_multiplier=-1).then_inc(bias_done, 1)
                    step[0] += 1
                    pool.wait_ge(bias_done, step[0])
            for n in range(2 * TT):
                t = n % 2
                next_rms(HD, qred_done, n + 1, slice(16 * t, 16 * t + 16))
            next_rms(P, ored_done, TT, slice(0, 8))
            norm_rms(2)
            ada_vector(8)
            ada_loop(1, 0, 9, 4)
            norm_rms(3)
            ada_loop(1, 4, 13, 5)
            for n, src in enumerate((pool_b, pool_scale)):
                if n == 0:
                    pool.wait_ge(x_done, 2 * TT)
                pool.dma_start(v_sb[:, n, :], row_bcast(src, D)).then_inc(pool_in, 16)
            pool.dma_start(avg[:, :, :, :], pool_avg).then_inc(avg_in, 16)
            norm_rms(4)
            norm_rms(5)

        @block.scalar
        def _(act):
            def split_hi(n, i=0):
                act.wait_ge(raw13_in[(n // 2) % 2], 32 * i + raw13_count(n // 2))
                if n >= 2:
                    act.wait_ge(unit_used, 4 * i + (n - 1))
                src, (hi, _) = unit_src(n)
                nc.scalar.activation(hi, src, ACT.Copy).then_inc(hi13_done, 1)

            def norm_squares(s):
                for t in range(TT):
                    if s == 0:
                        act.wait_ge(x_in_sem, 32)
                    else:
                        act.wait_ge(x_done, 2 * (s - 1) + t + 1)
                    nc.scalar.activation(xn[:, t, :], x[:, t, :], ACT.Square, accum_out=ss[:, t:t + 1]
                                         ).then_inc(ss_done, 1)

            def norm_out(s):
                g = NMOD * (s // 3) + 3 * (s % 3)
                act.wait_ge(acol_done, s + 1)
                for j in range(KT):
                    if j % 2 == 0:
                        act.wait_ge(xT_done, 4 * s + j // 2 + 1)
                    nc.scalar.activation(h32[:, j, :], ps[:, norm_bank(s, j), (j % 2) * 256:(j % 2) * 256 + 256],
                                         ACT.Identity, bias=modc[:, g, j:j + 1], scale=acol[:, s, j:j + 1]
                                         ).then_inc(h32_done, 1)

            def gate_copy(k, dst=gate[:, :]):
                act.wait_ge(gate_ps, k + 1)
                nc.scalar.activation(dst, ps[:, 6:8, :].rearrange("p b n -> p (b n)"), ACT.Copy
                                     ).then_inc(gate_ready, 1)

            def silu(Q, n, i4=0):
                act.wait_ge(unit_used, i4 + (n + 1))
                nc.scalar.activation(s_buf[:, Q % 2, :], ps[:, 4 + Q % 2, 0:256], ACT.Silu).then_inc(silu_done, 1)

            def u_high(Q, i4=0):
                act.wait_ge(u_done, i4 + (Q + 1))
                nc.scalar.activation(u_hi[:, Q % 2, :], u_buf[:, Q % 2, :], ACT.Copy).then_inc(uhi_done, 1)

            def w2_high(Q, i=0):
                act.wait_ge(raw2_in[Q % 2], 32 * i + 16 * (Q // 2 + 1))
                if Q >= 1:
                    act.wait_ge(w2_used, 4 * i + (Q + Q // NC))
                nc.scalar.activation(hi2[:, Q % 2, :], raw2[:, Q % 2, :], ACT.Copy).then_inc(hi2_done, 1)

            def ffn(f):
                Q0, n0 = NC * f, 2 * FFN_PAIR[f]
                w2_high(Q0)
                split_hi(n0 + 1)
                with act.Fori(0, 5) as i:
                    for q in range(1, 5):
                        silu(Q0 + q - 1, n0 + q - 1, 4 * i)
                        w2_high(Q0 + q, i)
                        u_high(Q0 + q - 1, 4 * i)
                        split_hi(n0 + q + 1, i)
                silu(Q0 + 20, n0 + 20)
                w2_high(Q0 + 21)
                u_high(Q0 + 20)
                silu(Q0 + 21, n0 + 21)
                u_high(Q0 + 21)
                gate_copy(SUB_OF_FFN[f])
                if f < 3:
                    split_hi(n0 + 22)

            act.dma_start(cond[:, :], c_col).then_inc(cond_done, 16)
            act.dma_start(adab[:, :, :], ada_bT).then_inc(adab_in, 16)
            act.dma_start(exch[:, :], exchange).then_inc(small_in, 16)
            act.dma_start(ngT[:, :, :], norm_gT).then_inc(small_in, 16)
            act.dma_start(gnorm[:, :, :].rearrange("p a b -> p (a b)"), row_bcast(a_qk_norm, 2 * HD)
                          ).then_inc(small_in, 16)
            act.dma_start(bnorm[:, :], b_qk_normT).then_inc(small_in, 16)
            act.dma_start(rope[:, :, :, :], rope_cs).then_inc(small_in, 16)
            act.dma_start(subln[:, :], row_bcast(a_subln, P)).then_inc(small_in, 16)
            act.dma_start(lamb[:, :, :].rearrange("p a b -> p (a b)"), row_bcast(a_lambda, 4 * HD)
                          ).then_inc(small_in, 16)
            act.wait_ge(cond_done, 16)
            nc.scalar.activation(cond[:, :], cond[:, :], ACT.Silu).then_inc(cond_done, 1)
            norm_squares(0)
            split_hi(0)
            norm_out(0)
            ffn(0)
            norm_squares(1)
            norm_out(1)
            act.wait_ge(lam_done, 1)
            nc.scalar.activation(lam[:, 2:4], lam[:, 0:2], ACT.Exp).then_inc(lam_done, 1)

            def win_evac(w):
                n = 2 * WIN_PAIR + w
                act.wait_ge(unit_used, n + 1)
                seg, half = WIN_SEGS[w]
                if seg in ("va", "vb"):
                    c0 = (512 if seg == "vb" else 0) + half * 256
                    dst = v_sb[:, :, c0:c0 + 256]
                else:
                    c0 = (512 if seg[0] == "k" else 0) + half * 256
                    dst = xn[:, :, c0:c0 + 256]
                    if seg == "qb" and half == 0:
                        act.wait_ge(tp_fill, 4)
                nc.scalar.activation(dst, ps[:, 4 + w % 2, :].rearrange("p (t n) -> p t n", t=TT), ACT.Copy
                                     ).then_inc(win_out, 1)

            tp = [0]

            def tp_evac(dst, scale=1.0):
                tp[0] += 1
                act.wait_ge(tp_fill, tp[0])
                nc.scalar.activation(dst, ps[:, (tp[0] - 1) % 2, :], ACT.Copy, scale=scale).then_inc(tp_out, 1)

            def qk_evac(ab):
                for b in range(4):
                    if ab == 1 and b == 0:
                        act.wait_ge(bnorm_done, 1)
                    tp_evac(qkT[:, 2 * b:2 * b + 2, :].rearrange("p b n -> p (b n)"),
                            1.0 if ab == 0 else bnorm[:, b // 2:b // 2 + 1])

            def squares(ab, t):
                if ab == 0:
                    act.wait_ge(win_out, 4)
                    if t == 1:
                        act.wait_ge(mod_done, 8)
                else:
                    act.wait_ge(win_out, 10)
                    act.wait_ge(qred_done, 2)
                nc.scalar.activation((gate, acc)[t][:, :], xn[:, t, :], ACT.Square).then_inc(sq_done, 1)

            def exps(u):
                act.wait_ge(nmx_done, u + 1)
                if u >= 4:
                    act.wait_ge(tp_fill, slot_free(u))
                for t in range(TT):
                    nc.scalar.activation(e_buf[:, u % 4, t, :], ps[:, 6 + u % 2, t * 256:t * 256 + 256], ACT.Exp,
                                         bias=nmx[:, u, t:t + 1], accum_out=esum[:, u, t:t + 1]).then_inc(exp_done, 1)

            def weights_evac(k):
                if k >= 2:
                    act.wait_ge(pv_done, k - 1)
                tp_evac(ptT[k % 2][:, :, :].rearrange("p a n -> p (a n)"))

            n0 = 2 * WIN_PAIR
            for w in range(12):
                h = w - 8
                if w == 7:
                    split_hi(n0 + 8)
                    qk_evac(0)
                if w >= 1:
                    win_evac(w - 1)
                if h >= 1:
                    weights_evac(h - 1)
                if w != 7:
                    split_hi(n0 + w + 1)
                if w == 4:
                    squares(0, 0)
                    squares(0, 1)
                if h >= 0:
                    exps(2 * h)
                    exps(2 * h + 1)
                if w == 10:
                    squares(1, 0)
                    squares(1, 1)
            win_evac(11)
            weights_evac(3)
            qk_evac(1)
            act.wait_ge(pv_done, A_HEADS)
            for t in range(TT):
                nc.scalar.activation(mix[:, t, 0:512], ps[:, 2 + t, :], ACT.Square).then_inc(osq_done, 1)
            split_hi(n0 + 13)

            def b_output(m):
                act.wait_ge(pv_done, A_HEADS + 4 * m + 4)
                nc.scalar.activation(hT_hi[:, 4 + 2 * m:6 + 2 * m, :].rearrange("p j n -> p (j n)"), ps[:, 2 + m, :],
                                     ACT.Copy).then_inc(mixb_hi, 1)

            for b in range(B_HEADS + 2):
                if b < B_HEADS:
                    exps(8 + b)
                if b >= 2:
                    weights_evac(2 + b)
                if b == 5:
                    for j2 in range(2):
                        tp_evac(gate[:, j2 * 512:j2 * 512 + 512])
                if b == 8:
                    b_output(0)
            b_output(1)
            act.wait_ge(hlo_done, HLO[1] + 8 + 4)
            gate_copy(1)
            for n in (36, 37, 38):
                split_hi(n)
            norm_squares(2)
            norm_out(2)
            ffn(1)
            norm_squares(3)
            norm_out(3)
            ffn(2)
            norm_squares(4)
            gate_copy(4, pool_gate)
            split_hi(2 * POOL_PAIR + 1)
            norm_out(4)
            g4 = NMOD + 3
            for j in range(KT):
                act.wait_ge(pool_ps, j // 2 + 1)
                nc.scalar.activation(pooled[:, j, :], ps[:, POOL_BANK[j // 2], (j % 2) * 256:(j % 2) * 256 + 256],
                                     ACT.Identity, bias=modc[:, g4, j:j + 1], scale=acol[:, 4, j:j + 1]
                                     ).then_inc(pooled_done, 1)
            split_hi(2 * FFN_PAIR[3])
            norm_squares(5)
            norm_out(5)
            ffn(3)

        @block.vector
        def _(dve):
            V = nc.vector

            def split_lo(n, i4=0, part=None):
                dve.wait_ge(hi13_done, i4 + (n + 1))
                src, (hi, lo) = unit_src(n)
                if part is not None:
                    half = src.shape[1] // 2
                    src, hi, lo = (v[:, part * half:(part + 1) * half] for v in (src, hi, lo))
                ins = V.tensor_tensor(lo, src, hi.bitcast(F32), ALU.subtract)
                if part != 0:
                    ins.then_inc(lo13_done, 1)

            def w2_low(Q, i4=0):
                dve.wait_ge(hi2_done, i4 + (Q + 1))
                V.tensor_tensor(lo2[:, Q % 2, :], raw2[:, Q % 2, :], hi2[:, Q % 2, :].bitcast(F32), ALU.subtract
                                ).then_inc(lo2_done, 1)

            def u_mul(Q, i4=0):
                dve.wait_ge(silu_done, i4 + (Q + 1))
                V.tensor_tensor(u_buf[:, Q % 2, :], s_buf[:, Q % 2, :], ps[:, 4 + Q % 2, 256:512], ALU.mult
                                ).then_inc(u_done, 1)

            def u_low(Q, i4=0):
                dve.wait_ge(uhi_done, i4 + (Q + 1))
                V.tensor_tensor(u_lo[:, Q % 2, :], u_buf[:, Q % 2, :], u_hi[:, Q % 2, :].bitcast(F32), ALU.subtract
                                ).then_inc(ulo_done, 1)

            def ada_tile(g, j, i=0, gates=0):
                n = KT * g + j
                if ADA_RING <= n < 2 * KT:
                    m = (n - ADA_RING) // 2
                    dve.wait_ge(first_in[m], 16)
                    w = first_ada[m][:, n % 2, :]
                else:
                    uses = 1 if n < ADA_RING else n // ADA_RING - 2
                    dve.wait_ge(ada_in[j % ADA_RING], 32 * i + 16 * uses)
                    w = ada[:, j % ADA_RING, :]
                if j == 0:
                    if gates:
                        dve.wait_ge(gate_ps, gates)
                    V.tensor_scalar(acc[:, :], w, cond[:, 0:1], None, ALU.mult).then_inc(ada_used, 1)
                else:
                    dve.wait_ge(ada_used, KT * i + (KT * g + j))
                    V.scalar_tensor_tensor(acc[:, :], w, cond[:, j:j + 1], acc[:, :], ALU.mult, ALU.add
                                           ).then_inc(ada_used, 1)

            def mod_out(g, i=0):
                dve.wait_ge(mod_ps, i + (g + 1))
                if isinstance(i, int):
                    dst, b = modc[:, g:g + 1, :], adab[:, g:g + 1, :]
                else:
                    dst, b = modc[:, bass.ds(i + g, 1), :], adab[:, bass.ds(i + g, 1), :]
                V.tensor_reduce(mraw[:, 0, :], ps[:, MOD_BANK:MOD_BANK + 2, :].rearrange("p b (k n) -> p (b k) n", n=P),
                                AX.X, ALU.add).then_inc(mod_red, 1)
                dve.wait_ge(mod_red, i + (g + 1))
                V.tensor_tensor(dst, mraw[:, :, :], b, ALU.add).then_inc(mod_done, 1)

            def diag(g, k, scale):
                dve.wait_ge(mod_done, g + 1)
                if k >= 1:
                    dve.wait_ge(gate_ps, k)
                for j in range(KT):
                    V.tensor_scalar(acc[:, j * P:(j + 1) * P], ident[:, :], modc[:, g, j:j + 1], scale,
                                    ALU.mult, ALU.mult).then_inc(diag_done, 1)

            def make_acol(s):
                g = NMOD * (s // 3) + 3 * (s % 3)
                dve.wait_ge(mod_done, g + 2)
                V.scalar_tensor_tensor(acol[:, s, :], modc[:, g + 1, :], 1.0, ngT[:, s, :], ALU.add, ALU.mult
                                       ).then_inc(acol_done, 1)

            def residual(s, k, sem_, at, y0=0):
                dve.wait_ge(gate_ready, k + 1)
                if y0:
                    dve.wait_ge(y0_done, y0)
                for t in range(TT):
                    if t == (1 if y0 else 0):
                        dve.wait_ge(sem_, at)
                    V.tensor_tensor(xn[:, t, :], ps[:, 2 * t:2 * t + 2, :].rearrange("p b n -> p (b n)"),
                                    gate[:, :], ALU.mult).then_inc(x_tmp, 1)
                    dve.wait_ge(x_tmp, 2 * (s - 1) + t + 1)
                    V.tensor_tensor(x[:, t, :], x[:, t, :], xn[:, t, :], ALU.add).then_inc(x_done, 1)

            def norm_scale(s):
                for t in range(TT):
                    dve.wait_ge(rstd_done, RS_AT[s] + t + 1)
                    V.tensor_scalar(xn[:, t, :], x[:, t, :], rstd[:, t:t + 1], None, ALU.mult).then_inc(xn_done, 1)

            def split_h(j2, src=h32):
                h, hi, lo = (v[:, 2 * j2:2 * j2 + 2, :].rearrange("p j n -> p (j n)") for v in (src, hT_hi, hT_lo))
                V.tensor_copy(hi, h).then_inc(hhi_done, 1)
                hhi_n[0] += 1
                dve.wait_ge(hhi_done, hhi_n[0])
                V.tensor_tensor(lo, h, hi.bitcast(F32), ALU.subtract).then_inc(hlo_done, 2)

            hhi_n = [0]

            def norm_split(s):
                for j2 in range(KT // 2):
                    dve.wait_ge(h32_done, H32[s] + 2 * j2 + 2)
                    split_h(j2)

            def norm(s, n=None):
                if n is not None:
                    split_lo(n, part=0)
                norm_scale(s)
                if n is not None:
                    split_lo(n, part=1)
                norm_split(s)

            def ffn(f, m0=None, turns=0, gates=0):
                Q0, n0 = NC * f, 2 * FFN_PAIR[f]
                w2_low(Q0)
                split_lo(n0 + 1)

                def body(i, with_ada):
                    for d in range(4):
                        Q = Q0 + 1 + d
                        u_mul(Q - 1, 4 * i)
                        if with_ada:
                            ada_tile(m0, 2 * d, i, gates)
                        u_low(Q - 1, 4 * i)
                        if with_ada:
                            ada_tile(m0, 2 * d + 1, i, gates)
                        w2_low(Q, 4 * i)
                        split_lo(n0 + d + 2, 4 * i)
                    if with_ada:
                        mod_out(m0, i)

                if turns:
                    with dve.Fori(0, turns) as i:
                        body(i, True)
                if turns == 0:
                    with dve.Fori(0, 5) as i:
                        body(i, False)
                u_mul(Q0 + 20)
                u_low(Q0 + 20)
                w2_low(Q0 + 21)
                diag(GATES[SUB_OF_FFN[f]], SUB_OF_FFN[f], 0.5)
                u_mul(Q0 + 21)
                u_low(Q0 + 21)

            V.memset(ones[:, :], 1.0).then_inc(setup_done, 1)
            V.memset(zeros[:, :], 0.0).then_inc(setup_done, 1)
            norm_scale(0)
            dve.wait_ge(cond_done, 17)
            for g in range(2):
                for j in range(KT):
                    ada_tile(g, j)
                if g == 0:
                    dve.wait_ge(adab_in, 16)
                else:
                    split_lo(0, part=0)
                mod_out(g)
            dve.wait_ge(small_in, 16 * 7)
            make_acol(0)
            split_lo(0, part=1)
            norm_split(0)
            ffn(0, m0=2, turns=5)
            V.tensor_scalar(bnorm[:, 0:1], bnorm[:, 0:1], SCALE, None, ALU.mult).then_inc(bnorm_done, 1)
            V.tensor_scalar(gnorm[:, 0, :], gnorm[:, 0, :], SCALE, None, ALU.mult).then_inc(setup_step, 1)
            dve.wait_ge(setup_step, 1)
            for cs in range(2):
                for t in range(TT):
                    V.tensor_tensor(rope_g[:, cs, t, :, :].rearrange("p q (h d) -> p (q h) d", d=32),
                                    gnorm[:, :, :].rearrange("p q (h d) -> p (q h) d", d=32),
                                    rope[:, cs, t, :].unsqueeze(1).to_broadcast([P, 4, 32]), ALU.mult
                                    ).then_inc(setup_step, 1)
            V.tensor_scalar(subln[:, :], subln[:, :], 1.0 - LAM0, None, ALU.mult).then_inc(setup_step, 1)
            V.tensor_tensor(lamb[:, 0:4:2, :], lamb[:, 0:4:2, :], lamb[:, 1:4:2, :], ALU.mult).then_inc(setup_step, 1)
            dve.wait_ge(setup_step, 7)
            V.tensor_reduce(lam[:, 0:2], lamb[:, 0:4:2, :], AX.X, ALU.add).then_inc(lam_done, 1)
            make_acol(1)
            residual(1, 0, w2_used, w2_count(NC - 1), y0=1)
            norm(1, 22)

            def qk_sums(t, ab):
                dve.wait_ge(sq_done, 2 * ab + t + 1)
                V.tensor_reduce(ss[:, 16 * t:16 * t + 16], (gate, acc)[t][:, :].rearrange("p (g d) -> p g d", d=HD),
                                AX.X, ALU.add).then_inc(qred_done, 1)

            def qk_norm(t, ab):
                dve.wait_ge(rstd_done, RS_AT[1] + 2 + 2 * ab + t + 1)
                qk = xn[:, t, :].rearrange("p (g d) -> p g d", d=HD)
                rs = rstd[:, 16 * t:16 * t + 16].unsqueeze(2).to_broadcast([P, 16, HD])
                if ab == 1:
                    V.tensor_tensor(qk, qk, rs, ALU.mult).then_inc(qk_done, 2)
                    return
                V.tensor_tensor(qk, qk, rs, ALU.mult).then_inc(qk_step, 1)
                dve.wait_ge(qk_step, 3 * t + 1)
                qk4 = xn[:, t, :].rearrange("p (s h d) -> p s h d", s=2, h=8)
                for cs in range(2):
                    V.tensor_tensor(mix[:, cs, :].rearrange("p (s h d) -> p s h d", s=2, h=8), qk4,
                                    rope_g[:, cs, t, :, :].unsqueeze(2).to_broadcast([P, 2, 8, HD]), ALU.mult
                                    ).then_inc(qk_step, 1)
                dve.wait_ge(qk_step, 3 * t + 3)
                xc = mix[:, 0, :].rearrange("p (g d) -> p g d", d=HD)
                xs = mix[:, 1, :].rearrange("p (g d) -> p g d", d=HD)
                V.tensor_tensor(qk[:, :, 0:32], xc[:, :, 0:32], xs[:, :, 32:64], ALU.subtract).then_inc(qk_done, 1)
                V.tensor_tensor(qk[:, :, 32:64], xs[:, :, 0:32], xc[:, :, 32:64], ALU.add).then_inc(qk_done, 1)

            def row_max(u):
                dve.wait_ge(score_done, u + 1)
                V.tensor_reduce(nmx[:, u, :], ps[:, 6 + u % 2, :].rearrange("p (t n) -> p t n", t=TT), AX.X, ALU.max
                                ).then_inc(nmx_tmp, 1)
                dve.wait_ge(nmx_tmp, u + 1)
                V.tensor_scalar(nmx[:, u, :], nmx[:, u, :], -1.0, None, ALU.mult).then_inc(nmx_done, 1)

            def combine(h):
                dve.wait_ge(exp_done, 2 * (2 * h + 2))
                V.reciprocal(erec[:, 2 * h:2 * h + 2, :], esum[:, 2 * h:2 * h + 2, :]).then_inc(erec_done, 1)
                dve.wait_ge(erec_done, 2 * h + 1)
                V.tensor_scalar(erec[:, 2 * h + 1, :], erec[:, 2 * h + 1, :], lam[:, 0:1], None, ALU.mult
                                ).then_inc(erec_done, 1)
                dve.wait_ge(erec_done, 2 * h + 2)
                a, b = (2 * h) % 4, (2 * h + 1) % 4
                for t in range(TT):
                    V.tensor_scalar(e_buf[:, b, t, :], e_buf[:, b, t, :], erec[:, 2 * h + 1, t:t + 1], None, ALU.mult
                                    ).then_inc(comb_tmp, 1)
                for t in range(TT):
                    dve.wait_ge(comb_tmp, 2 * h + t + 1)
                    V.scalar_tensor_tensor(e_buf[:, a, t, :], e_buf[:, a, t, :], erec[:, 2 * h, t:t + 1],
                                           e_buf[:, b, t, :], ALU.mult, ALU.add).then_inc(comb_done, 1)

            dve.wait_ge(lam_done, 2)
            V.tensor_tensor(lam[:, 0:1], lam[:, 3:4], lam[:, 2:3], ALU.subtract).then_inc(lam_done, 1)
            dve.wait_ge(lam_done, 3)
            V.tensor_scalar(lam[:, 0:1], lam[:, 0:1], -LAM0, None, ALU.add).then_inc(lam_done, 1)
            dve.wait_ge(lam_done, 4)
            n0 = 2 * WIN_PAIR
            for w in range(12):
                h = w - 8
                if h >= 0:
                    row_max(2 * h)
                    row_max(2 * h + 1)
                split_lo(n0 + w + 1)
                if w < 4:
                    for j in (2 * w, 2 * w + 1):
                        ada_tile(7, j, gates=1)
                if w == 4:
                    mod_out(7)
                    qk_sums(0, 0)
                    qk_sums(1, 0)
                if w in (5, 6):
                    qk_norm(w - 5, 0)
                if h >= 0:
                    combine(h)
                if w == 10:
                    qk_sums(0, 1)
                    qk_sums(1, 1)
            qk_norm(0, 1)
            qk_norm(1, 1)
            diag(GATES[1], 1, 1.0)

            def a_output(t):
                dve.wait_ge(osq_done, t + 1)
                V.tensor_reduce(ss[:, 4 * t:4 * t + 4], mix[:, t, 0:512].rearrange("p (h d) -> p h d", d=P), AX.X,
                                ALU.add).then_inc(ored_done, 1)

            def a_scale(t):
                dve.wait_ge(rstd_done, RS_AT[1] + 2 + 4 + 1)
                m = mix[:, t, 0:512].rearrange("p (h d) -> p h d", d=P)
                V.tensor_tensor(m, ps[:, 2 + t, :].rearrange("p (h d) -> p h d", d=P),
                                rstd[:, 4 * t:4 * t + 4].unsqueeze(2).to_broadcast([P, 4, P]), ALU.mult
                                ).then_inc(omul_done, 1)
                dve.wait_ge(omul_done, t + 1)
                V.tensor_tensor(m, m, subln[:, :].unsqueeze(1).to_broadcast([P, 4, P]), ALU.mult
                                ).then_inc(mix_done, 1)

            def normalise(b):
                u = 2 * A_HEADS + b
                dve.wait_ge(exp_done, 2 * (u + 1))
                V.reciprocal(erec[:, u, :], esum[:, u, :]).then_inc(erec_done, 1)
                dve.wait_ge(erec_done, 2 * A_HEADS + b + 1)
                for t in range(TT):
                    V.tensor_scalar(e_buf[:, u % 4, t, :], e_buf[:, u % 4, t, :], erec[:, u, t:t + 1], None, ALU.mult
                                    ).then_inc(en_done, 1)

            def b_output(m):
                dve.wait_ge(mixb_hi, m + 1)
                hi, lo = (v[:, 4 + 2 * m:6 + 2 * m, :].rearrange("p j n -> p (j n)") for v in (hT_hi, hT_lo))
                V.tensor_tensor(lo, ps[:, 2 + m, :], hi.bitcast(F32), ALU.subtract).then_inc(hlo_done, 2)

            a_output(0)
            a_output(1)
            split_lo(n0 + 13)
            for b in range(B_HEADS + 1):
                if b < B_HEADS:
                    row_max(8 + b)
                if b >= 1:
                    normalise(b - 1)
                if b == 1:
                    a_scale(0)
                    a_scale(1)
                if b == 7:
                    for j2 in range(2):
                        dve.wait_ge(tp_out, TP_MIX + j2 + 1)
                        split_h(j2, gate[:, :].rearrange("p (j n) -> p j n", n=SEQ))
            b_output(0)
            b_output(1)
            for n in (36, 37, 38):
                split_lo(n)
            make_acol(2)
            residual(2, 1, unit_used, 2 * WOUT_PAIR + 4)
            norm(2)
            ffn(1, m0=8, turns=5, gates=2)
            make_acol(3)
            residual(3, 2, w2_used, w2_count(2 * NC - 1), y0=2)
            norm(3, 2 * FFN_PAIR[2])
            ffn(2, m0=13, turns=5, gates=3)
            make_acol(4)
            diag(GATES[4], 4, 1.0)
            residual(4, 3, w2_used, w2_count(3 * NC - 1), y0=3)
            split_lo(2 * POOL_PAIR)
            norm_scale(4)

            split_lo(2 * POOL_PAIR + 1)
            dve.wait_ge(pool_in, 32)
            dve.wait_ge(gate_ready, 5)
            V.tensor_tensor(gate[:, :], pool_gate, v_sb[:, 1, :], ALU.mult).then_inc(pool_step, 1)
            dve.wait_ge(pool_step, 1)
            V.tensor_tensor(v_sb[:, 0, :], v_sb[:, 0, :], gate[:, :], ALU.mult).then_inc(pool_step, 1)
            dve.wait_ge(pool_step, 2)
            for t in range(TT):
                V.tensor_tensor(x[:, t, :], x[:, t, :], v_sb[:, 0, :], ALU.add).then_inc(pool_step, 1)
            for j2 in range(KT // 2):
                dve.wait_ge(h32_done, H32[4] + 2 * j2 + 2)
                dve.wait_ge(pooled_done, 2 * j2 + 2)
                d = pooled[:, 2 * j2:2 * j2 + 2, :]
                V.tensor_tensor(d, d, h32[:, 2 * j2:2 * j2 + 2, :], ALU.subtract).then_inc(diff_done, 1)
                dve.wait_ge(diff_done, j2 + 1)
                split_h(j2, pooled)
            dve.wait_ge(pool_step, 4)
            make_acol(5)
            residual(5, 4, unit_used, 2 * POOL_PAIR + 2)
            norm(5, 2 * FFN_PAIR[3])
            ffn(3)
            residual(6, 5, w2_used, w2_count(4 * NC - 1), y0=4)

        @block.tensor
        def _(pe):
            mm = nc.tensor.matmul

            def norm(s):
                for t in range(TT):
                    pe.wait_ge(xn_done, 2 * s + t + 1)
                    for j in range(KT):
                        c0 = (j % 2) * 256 + t * P
                        ins = nc.tensor.transpose(ps[:, norm_bank(s, j), c0:c0 + P], xn[:, t, j * P:(j + 1) * P],
                                                  ident[:, :])
                        if t == TT - 1 and j % 2:
                            ins.then_inc(xT_done, 1)

            def three(out, pairs, first, last):
                for m, (a, b) in enumerate(pairs):
                    ins = mm(out, a, b, start=first and m == 0, stop=last and m == len(pairs) - 1)
                return ins

            def w13(s, Q, n, i4=0, hs=None):
                pe.wait_ge(lo13_done, i4 + (n + 1))
                for ab in range(2):
                    for k in range(KT):
                        if hs is not None and ab == 0:
                            pe.wait_ge(hlo_done, hs + k + 1)
                        w0 = (ab * KT + k) * P
                        wh, wl = hi13[:, n % 2, w0:w0 + P], lo13[:, n % 2, w0:w0 + P]
                        hh, hl = hT_hi[:, k, :], hT_lo[:, k, :]
                        ins = three(ps[:, 4 + Q % 2, ab * 256:ab * 256 + 256], ((wh, hh), (wh, hl), (wl, hh)),
                                    k == 0, k == KT - 1)
                ins.then_inc(unit_used, 1)

            def w2(Q, i4=0, tiles=range(TT), last=False, done=w2_used):
                pe.wait_ge(ulo_done, i4 + (Q + 1))
                pe.wait_ge(lo2_done, i4 + (Q + 1))
                p = Q % 2
                for t in tiles:
                    uh, ul = u_hi[:, p, t * P:(t + 1) * P], u_lo[:, p, t * P:(t + 1) * P]
                    for h in range(2):
                        wh, wl = hi2[:, p, h * 512:h * 512 + 512], lo2[:, p, h * 512:h * 512 + 512]
                        mm(ps[:, 2 * t + h, :], uh, wh, start=False, stop=False)
                        mm(ps[:, 2 * t + h, :], uh, wl, start=False, stop=False)
                    for h in range(2):
                        wh = hi2[:, p, h * 512:h * 512 + 512]
                        ins = mm(ps[:, 2 * t + h, :], ul, wh, start=False, stop=last)
                if done is not None:
                    ins.then_inc(done, 1)

            def mod_sum(g, i=0):
                pe.wait_ge(ada_used, KT * i + KT * (g + 1))
                if g >= 1:
                    pe.wait_ge(mod_done, i + g)
                for j in range(KT):
                    c0 = (j % 4) * P
                    ins = nc.tensor.transpose(ps[:, MOD_BANK + j // 4, c0:c0 + P], acc[:, j * P:(j + 1) * P],
                                              ident[:, :])
                ins.then_inc(mod_ps, 1)

            def gate_row(k, mods):
                pe.wait_ge(diag_done, KT * (k + 1))
                pe.wait_ge(mod_done, mods)
                for h in range(2):
                    ins = mm(ps[:, 6 + h, :], ones[:, :], acc[:, h * 512:h * 512 + 512], start=True, stop=True)
                ins.then_inc(gate_ps, 1)

            def ffn(f, m0=None, turns=0, mods=0):
                s = SUB_OF_FFN[f]
                Q0, n0 = NC * f, 2 * FFN_PAIR[f]
                w13(s, Q0, n0, hs=HLO[s])
                for b in range(4):
                    ins = mm(ps[:, b, :], zeros[:, :], zeros[:, 0:1].to_broadcast([P, 512]), start=True, stop=False)
                ins.then_inc(w2_used, 1)

                def body(i, with_mod):
                    i4 = 4 * i
                    for d in range(4):
                        Q = Q0 + 1 + d
                        w13(s, Q, n0 + 1 + d, i4)
                        if with_mod and d == 3:
                            mod_sum(m0, i)
                        w2(Q - 1, i4)

                if turns:
                    with pe.Fori(0, turns) as i:
                        body(i, True)
                if turns == 0:
                    with pe.Fori(0, 5) as i:
                        body(i, False)
                w13(s, Q0 + 21, n0 + 21)
                w2(Q0 + 20, tiles=[0], done=None)
                gate_row(s, mods)
                w2(Q0 + 21, tiles=[0], last=True, done=y0_done)
                w2(Q0 + 20, tiles=[1])
                w2(Q0 + 21, tiles=[1], last=True)

            pe.wait_ge(setup_done, 2)
            pe.wait_ge(ident_in, 16)
            norm(0)
            mod_sum(0)
            mod_sum(1)
            ffn(0, m0=2, turns=5, mods=7)
            norm(1)

            def proj(n, hs=None, out_of=None):
                pe.wait_ge(lo13_done, n + 1)
                for t in range(TT):
                    for k in range(KT):
                        if hs is not None and t == 0:
                            pe.wait_ge(hlo_done, hs + k + 1)
                        tok = slice(t * P, (t + 1) * P)
                        hh, hl = hT_hi[:, k, tok], hT_lo[:, k, tok]
                        wh, wl = hi13[:, n % 2, k * 256:k * 256 + 256], lo13[:, n % 2, k * 256:k * 256 + 256]
                        ins = three(out_of(t), ((hh, wh), (hh, wl), (hl, wh)), k == 0, k == KT - 1)
                ins.then_inc(unit_used, 1)

            tp = [0]

            def tp_bank():
                n = tp[0]
                if n >= 2:
                    pe.wait_ge(tp_out, n - 1)
                tp[0] += 1
                return n % 2

            def qk_transpose(ab):
                pe.wait_ge(qk_done, 4 * ab + 4)
                for b2 in range(4):
                    bank = tp_bank()
                    for b in range(2):
                        for t in range(TT):
                            blk = 2 * b2 + b
                            ins = nc.tensor.transpose(ps[:, bank, b * 256 + t * P:b * 256 + t * P + P],
                                                      xn[:, t, blk * P:(blk + 1) * P], ident[:, :])
                    ins.then_inc(tp_fill, 1)

            def scores(u, tp_need):
                pe.wait_ge(tp_out, tp_need)
                if u >= 2:
                    pe.wait_ge(exp_done, 2 * (u - 1))
                v = u % (2 * A_HEADS)
                rows = slice((v % 2) * 64, (v % 2) * 64 + 64)
                for t in range(TT):
                    ins = mm(ps[:, 6 + u % 2, t * 256:t * 256 + 256], qkT[rows, v // 2, t * P:(t + 1) * P],
                             qkT[rows, 4 + v // 2, :], start=True, stop=u < 2 * A_HEADS)
                    if u >= 2 * A_HEADS:
                        ins = mm(ps[:, 6 + u % 2, t * 256:t * 256 + 256], exch[:, :],
                                 bias[:, t, v, :, :].rearrange("p r c -> p (r c)"), start=False, stop=True)
                ins.then_inc(score_done, 1)

            def weights_transpose(k):
                bank = tp_bank()
                if k < A_HEADS:
                    pe.wait_ge(comb_done, 2 * (k + 1))
                    slot = (2 * k) % 4
                else:
                    u = 2 * A_HEADS + k - A_HEADS
                    pe.wait_ge(en_done, 2 * (k - A_HEADS + 1))
                    slot = u % 4
                for kt in range(2):
                    for t in range(TT):
                        ins = nc.tensor.transpose(ps[:, bank, kt * 256 + t * P:kt * 256 + t * P + P],
                                                  e_buf[:, slot, t, kt * P:(kt + 1) * P], ident[:, :])
                ins.then_inc(tp_fill, 1)

            def values(k):
                pe.wait_ge(tp_out, TP_HEAD(k) + 1)
                if k == 0:
                    pe.wait_ge(win_out, 6)
                if k == A_HEADS:
                    pe.wait_ge(win_out, 12)
                    pe.wait_ge(omul_done, 2)
                if k < A_HEADS:
                    for t in range(TT):
                        for kt in range(2):
                            ins = mm(ps[:, 2 + t, k * P:(k + 1) * P], ptT[k % 2][:, kt, t * P:(t + 1) * P],
                                     v_sb[:, kt, k * P:(k + 1) * P], start=kt == 0, stop=kt == 1)
                else:
                    b = k - A_HEADS
                    rows = slice((b % 2) * HD, (b % 2) * HD + HD)
                    dst = ps[rows, 2 + b // 4, (b // 2 % 2) * 256:(b // 2 % 2) * 256 + 256]
                    for kt in range(2):
                        ins = mm(dst, v_sb[:, kt, 512 + b * HD:512 + (b + 1) * HD], ptT[k % 2][:, kt, :],
                                 start=kt == 0, stop=kt == 1)
                ins.then_inc(pv_done, 1)

            n0 = 2 * WIN_PAIR
            for w in range(12):
                h = w - 8
                if w >= 2:
                    pe.wait_ge(win_out, w - 1)
                if w == 7:
                    qk_transpose(0)
                if h == 0:
                    pe.wait_ge(mod_done, 8)
                if h >= 0:
                    scores(2 * h, 4)
                    scores(2 * h + 1, 4)
                proj(n0 + w, hs=HLO[1] if w == 0 else None,
                     out_of=lambda t, w=w: ps[:, 4 + w % 2, t * 256:t * 256 + 256])
                if w == 3:
                    mod_sum(7)
                if h >= 0:
                    weights_transpose(h)
                if h >= 1:
                    values(h - 1)
            values(3)
            qk_transpose(1)
            pe.wait_ge(bias_done, 8)
            for b in range(B_HEADS + 3):
                if b < B_HEADS:
                    scores(8 + b, 12)
                if 2 <= b < B_HEADS + 2:
                    weights_transpose(2 + b)
                if b == 5:
                    pe.wait_ge(mix_done, 2)
                    for j2 in range(2):
                        bank = tp_bank()
                        for jj in range(2):
                            for t in range(TT):
                                j = 2 * j2 + jj
                                ins = nc.tensor.transpose(ps[:, bank, jj * 256 + t * P:jj * 256 + t * P + P],
                                                          mix[:, t, j * P:(j + 1) * P], ident[:, :])
                        ins.then_inc(tp_fill, 1)
                if b >= 3:
                    values(1 + b)
            pe.wait_ge(exp_done, 2 * (2 * A_HEADS + B_HEADS))
            gate_row(1, 8)
            for v in range(4):
                proj(2 * WOUT_PAIR + v, hs=HLO[1] + 8 if v == 0 else None,
                     out_of=lambda t, v=v: ps[:, 2 * t + v // 2, (v % 2) * 256:(v % 2) * 256 + 256])
            norm(2)
            ffn(1, m0=8, turns=5, mods=13)
            norm(3)
            ffn(2, m0=13, turns=5, mods=18)
            pe.wait_ge(gate_ready, 4)
            gate_row(4, 18)
            norm(4)
            pe.wait_ge(avg_in, 16)
            for j in range(KT):
                if j == 4:
                    pe.wait_ge(gate_ready, 5)
                for kt in range(TT):
                    ins = mm(ps[:, POOL_BANK[j // 2], (j % 2) * 256:(j % 2) * 256 + 256],
                             xn[:, kt, j * P:(j + 1) * P], avg[:, j // 2, kt, :], start=kt == 0, stop=kt == 1)
                if j % 2:
                    ins.then_inc(pool_ps, 1)

            for g in range(4):
                n = 2 * POOL_PAIR + g // 2
                pe.wait_ge(lo13_done, n + 1)
                pe.wait_ge(hlo_done, HLO[4] + 2 * g + 2)
                for t in range(TT):
                    for kk in range(2):
                        k = 2 * g + kk
                        tok = slice(t * P, (t + 1) * P)
                        c0 = ((2 * g + kk) % 4) * 256
                        hh, hl = hT_hi[:, k, tok], hT_lo[:, k, tok]
                        wh, wl = hi13[:, n % 2, c0:c0 + 256], lo13[:, n % 2, c0:c0 + 256]
                        dst = ps[:, 2 * t + g // 2, (g % 2) * 256:(g % 2) * 256 + 256]
                        ins = three(dst, ((hh, wh), (hh, wl), (hl, wh)), kk == 0, kk == 1)
                if g % 2:
                    ins.then_inc(unit_used, 1)
            norm(5)
            ffn(3, mods=18)


def kernel(**inputs):
    import concourse.bacc as bacc
    from concourse.bass_utils import run_bass_kernel_spmd

    a = {k: np.ascontiguousarray(v) for k, v in inputs.items()}
    a["c"] = np.ascontiguousarray(a["c"].reshape(KT, P).T)
    a["ada_b"] = np.ascontiguousarray(a["ada_b"].reshape(2 * NMOD, KT, P).transpose(2, 0, 1))
    a["norm_g"] = np.ascontiguousarray(a["norm_g"].reshape(6, KT, P).transpose(2, 0, 1))
    a["b_qk_norm"] = np.ascontiguousarray(np.tile(a["b_qk_norm"][0].T, (2, 1)))
    inv = np.float32(10000.0) ** (-np.arange(0, HD, 2, dtype=np.float32) / np.float32(HD))
    ang = np.arange(SEQ, dtype=np.float32)[:, None] * inv[None, :]
    table = np.stack([np.cos(ang), np.sin(ang)]).astype(np.float32)
    a["rope_cs"] = np.ascontiguousarray(table.reshape(2, TT, P, HD // 2).transpose(2, 0, 1, 3))
    t = np.arange(SEQ)
    avg = []
    for w in WINDOWS:
        lo, hi = np.clip(t - w // 2, 0, SEQ), np.clip(t - w // 2 + w, 0, SEQ)
        avg.append(((t[:, None] >= lo) & (t[:, None] < hi)) / (hi - lo))
    avg = np.stack(avg, axis=1).astype(np.float32)
    a["pool_avg"] = np.ascontiguousarray(avg.reshape(TT, P, 4, SEQ).transpose(1, 2, 0, 3))
    a["identity"] = np.eye(P, dtype=np.float32)
    a["exchange"] = np.ascontiguousarray(a["identity"].reshape(P, 2, P // 2)[:, :, ::-1].reshape(P, P))

    nc = bacc.Bacc("TRN2", target_bir_lowering=False, num_devices=1)
    order = ["x", "c", "ada_w", "ada_b", "norm_g", "ff_w13", "ff_w2", "w_in", "w_out", "a_qk_norm",
             "a_lambda", "a_subln", "b_qk_norm", "b_rpb", "pool_w", "pool_b", "pool_scale",
             "rope_cs", "pool_avg", "identity", "exchange"]
    arrays, args = {}, []
    for name in order:
        arrays[f"in_{name}"] = a[name]
        args.append(nc.dram_tensor(f"in_{name}", a[name].shape, mybir.dt.from_np(a[name].dtype),
                                   kind="ExternalInput").ap())
    out = nc.dram_tensor("out_dram", (1, SEQ, D), F32, kind="ExternalOutput").ap()
    build_program(nc, *args, out)
    r = run_bass_kernel_spmd(nc, [arrays], core_ids=[0])
    return r.results[0]["out_dram"]
```

```python
import math
from contextlib import ExitStack

import numpy as np

import concourse.bass as bass
from concourse import mybir

P = 128
D = 1024
SEQ = 256
TT = SEQ // P
KT = D // P
DFF = 2816
NC = DFF // P
NMOD = 9
HD = 64
A_HEADS = 4
B_HEADS = 8
GRID_W = 64
ROWS = SEQ // GRID_W
NA_ROWS, NA_COLS = 8, 16
EPS = 1e-6
NEG = -1e30
LAM0 = 0.8 - 0.6 * math.exp(0.0)
SCALE = HD ** -0.5
WINDOWS = (2, 4, 8, 16)

F32 = mybir.dt.float32
F32R = mybir.dt.float32r
ACT = mybir.ActivationFunctionType
ALU = mybir.AluOpType
AX = mybir.AxisListType

FFN_PAIR = [0, 19, 30, 42]
WIN_PAIR, WOUT_PAIR, POOL_PAIR = 11, 17, 41
ADA_RING = 4
SUB_OF_FFN = [0, 2, 3, 5]
FIRST_BANK = 7
MIX_Y_BANK = (4, 2)
GATES = [NMOD * (s // 3) + 3 * (s % 3) + 2 for s in range(6)]
MOD_BANK = 6
H32 = [0, 8, 16, 24, 32, 40]
HLO = [0, 8, 24, 32, 40, 48]
RS_AT = [0, 2, 9, 11, 13, 15]
POOL_BANK = [2, 3, 6, 7]
WIN_COLS = [0, 1, 2, 5, 3, 4]
WIN_SEGS = [(seg, half) for seg in ("qa", "ka", "va", "vb", "qb", "kb") for half in range(2)]
TP_MIX = (16, 18)


def norm_bank(s, j):
    return ([5, 0, 1, 2] if s == 0 else [5, 0, 1, 4] if s == 4 else [5, 6, 0, 1])[j // 2]


def tp_head(k):
    return 4 + k + sum(k >= first for first in (3, 3, 4, 4, 8, 9))


def slot_free(u):
    before = u - 4
    head = before // 2 if before < 2 * A_HEADS else before - 2 * A_HEADS + A_HEADS
    return tp_head(head) + 1


def w2_count(Q):
    return Q + Q // NC + 2


def row_bcast(src, n):
    return bass.AP(tensor=src.tensor, offset=src.offset, ap=[[0, P], [1, n]])


def build_program(nc, x_in, c_col, ada_w, ada_bT, norm_gT, ff_w13, ff_w2, w_in, w_out, a_qk_norm,
                  a_lambda, a_subln, b_qk_normT, b_rpb, pool_w, pool_b, pool_scale,
                  rope_cs, pool_avg, identity, exchange, out):
    ctx = ExitStack()
    with ctx:
        def sb(name, shape, dt=F32):
            return ctx.enter_context(nc.sbuf_tensor(name, shape, dt))

        def sem(name):
            return ctx.enter_context(nc.semaphore(name))

        raw13 = sb("raw13", [P, 2, 2, KT, 256])
        raw2 = sb("raw2", [P, 2, D])
        hi13 = sb("hi13", [P, 2, 2048], F32R)
        lo13 = sb("lo13", [P, 2, 2048], F32R)
        hi2 = sb("hi2", [P, 2, D], F32R)
        lo2 = sb("lo2", [P, 2, D], F32R)
        ada = sb("ada", [P, ADA_RING, D])
        acc = sb("acc", [P, D])
        x = sb("x", [P, TT, D])
        xn = sb("xn", [P, TT, D])
        hT_hi = sb("hT_hi", [P, KT, SEQ], F32R)
        hT_lo = sb("hT_lo", [P, KT, SEQ], F32R)
        gate = sb("gate", [P, D])
        s_buf = sb("s_buf", [P, 2, SEQ])
        u_buf = sb("u_buf", [P, 2, SEQ])
        u_hi = sb("u_hi", [P, 2, SEQ], F32R)
        u_lo = sb("u_lo", [P, 2, SEQ], F32R)
        arena = sb("arena", [P, 12288])
        bias = arena[:, 0:4096].rearrange("p (t h r c) -> p t h r c", t=TT, h=B_HEADS, r=ROWS)
        qkT = arena[:, 4096:6144].rearrange("p (b n) -> p b n", b=8)
        h32 = qkT
        v_sb = arena[:, 6144:8192].rearrange("p (t n) -> p t n", t=TT)
        mix = arena[:, 8192:10240].rearrange("p (t n) -> p t n", t=TT)
        pooled = arena[:, 0:2048].rearrange("p (j n) -> p j n", j=KT)
        avg = arena[:, 2048:4096].rearrange("p (w t n) -> p w t n", w=4, t=TT)
        pool_gate = mix[:, 0, :]
        e_buf = arena[:, 10240:12288].rearrange("p (s t n) -> p s t n", s=4, t=TT)
        modc = sb("modc", [P, 2 * NMOD, KT])
        mraw = sb("mraw", [P, 1, KT])
        adab = sb("adab", [P, 2 * NMOD, KT])
        ngT = sb("ngT", [P, 6, KT])
        acol = sb("acol", [P, 6, KT])
        cond = sb("cond", [P, KT])
        ident = sb("ident", [P, P])
        ones = sb("ones", [P, P])
        exch = sb("exch", [P, P])
        neg_half = sb("neg_half", [P, 32])
        ss = sb("ss", [P, 32])
        rstd = sb("rstd", [P, 32])
        gnorm = sb("gnorm", [P, 2, HD])
        bnorm = sb("bnorm", [P, 2])
        rope = arena[:, 10240:10368].rearrange("p (c t d) -> p c t d", c=2, t=TT)
        lamb = arena[:, 10368:10624].rearrange("p (a d) -> p a d", a=4)
        subln = sb("subln", [P, P])
        lam = sb("lam", [P, 4])
        nmx = sb("nmx", [P, 16, TT])
        esum = sb("esum", [P, 16, TT])
        erec = sb("erec", [P, 16, TT])
        rope_g = sb("rope_g", [P, 2, TT, 2, HD])
        ps = ctx.enter_context(nc.psum_tensor("ps", [P, 8, 512], F32))

        first_ada = [raw13[:, 1, m, :, :].rearrange("p (a k) n -> p a (k n)", a=2) for m in range(2)]
        first_ada += [arena[:, c:c + 2 * D].rearrange("p (a n) -> p a n", a=2) for c in (0, 2 * D, 6 * D, 8 * D)]

        def win_ps(w, t):
            return ps[:, FIRST_BANK, 0:256] if (w, t) == (0, 1) else ps[:, 4 + w % 2, t * 256:t * 256 + 256]

        def b_ps(Q, first):
            return ps[:, FIRST_BANK, 0:256] if first else ps[:, 4 + Q % 2, 256:512]

        def acc_of(g):
            return xn[:, 0, :] if g == 1 else acc[:, :]

        ptT = [s_buf, u_buf]

        raw13_in = [sem(f"raw13_in{i}") for i in range(2)]
        raw2_in = [sem(f"raw2_in{i}") for i in range(2)]
        first_unit_in = sem("first_unit_in")
        first_in = [sem(f"first_in{i}") for i in range(6)]
        ada_in = [sem(f"ada_in{i}") for i in range(ADA_RING)]
        hi13_done, lo13_done, unit_used = sem("hi13_done"), sem("lo13_done"), sem("unit_used")
        hi2_done, lo2_done, w2_used = sem("hi2_done"), sem("lo2_done"), sem("w2_used")
        y0_done, y1_half = sem("y0_done"), sem("y1_half")
        x_half = sem("x_half")
        silu_done, u_done = sem("silu_done"), sem("u_done")
        uhi_done, ulo_done = sem("uhi_done"), sem("ulo_done")
        ada_used, mod_ps, mod_red, mod_done = sem("ada_used"), sem("mod_ps"), sem("mod_red"), sem("mod_done")
        diag_done, gate_ps, gate_ready = sem("diag_done"), sem("gate_ps"), sem("gate_ready")
        x_tmp, x_done = sem("x_tmp"), sem("x_done")
        ss_done, rstd_tmp, rstd_done, xn_done = sem("ss_done"), sem("rstd_tmp"), sem("rstd_done"), sem("xn_done")
        xT_done, acol_done = sem("xT_done"), sem("acol_done")
        h32_done, hhi_done, hlo_done = sem("h32_done"), sem("hhi_done"), sem("hlo_done")
        ident_in, adab_in = sem("ident_in"), sem("adab_in")
        small_in, x_in_sem, cond_done = sem("small_in"), sem("x_in_sem"), sem("cond_done")
        setup_done, half_set, bias_in, bias_done = sem("setup_done"), sem("half_set"), sem("bias_in"), sem("bias_done")
        lam_done, setup_step = sem("lam_done"), sem("setup_step")
        win_out = sem("win_out")
        sq_done, qred_done, qk_step, qk_done = sem("sq_done"), sem("qred_done"), sem("qk_step"), sem("qk_done")
        tp_fill, tp_out = sem("tp_fill"), sem("tp_out")
        score_done, nmx_tmp, nmx_done, exp_done = sem("score_done"), sem("nmx_tmp"), sem("nmx_done"), sem("exp_done")
        bnorm_done, en_done, mixb_hi = sem("bnorm_done"), sem("en_done"), sem("mixb_hi")
        erec_done, comb_tmp, comb_done, pv_done = sem("erec_done"), sem("comb_tmp"), sem("comb_done"), sem("pv_done")
        osq_done, ored_done, omul_done, mix_done = sem("osq_done"), sem("ored_done"), sem("omul_done"), sem("mix_done")
        pool_in, avg_in, pool_step = sem("pool_in"), sem("avg_in"), sem("pool_step")
        pool_ps, pooled_done, diff_done = sem("pool_ps"), sem("pooled_done"), sem("diff_done")
        out_sem = sem("out_sem")

        def raw13_count(pair):
            return 32 * (pair // 2 + 1)

        w13_v = [ff_w13[f // 2, f % 2].rearrange("(k p) n -> p k n", p=P) for f in range(4)]
        w2_v = [ff_w2[f // 2, f % 2].rearrange("(c p) n -> p c n", p=P) for f in range(4)]
        win_v = w_in[0].rearrange("(k p) n -> p k n", p=P)
        wout_v = w_out[0].rearrange("(k p) n -> p k n", p=P)
        pw_v = pool_w[0].rearrange("g (k p) n -> p (g k) n", p=P)
        ada_v = [ada_w[l].rearrange("(j p) n -> p j n", p=P) for l in range(2)]
        out_v = out[0].rearrange("(t p) n -> p t n", p=P)
        x_v = x_in[0].rearrange("(t p) n -> p t n", p=P)

        def unit_src(n):
            pair, half = n // 2, n % 2
            slot = pair % 2
            for f in range(4):
                if FFN_PAIR[f] <= pair < FFN_PAIR[f] + 11:
                    src = raw13[:, slot, :, :, half * P:half * P + P].rearrange("p h k n -> p (h k) n")
                    return src, [t[:, half, :].rearrange("p (a n) -> p a n", n=P) for t in (hi13, lo13)]
            if pair == POOL_PAIR:
                return (raw13[:, slot, half, 0:4, :].rearrange("p k n -> p (k n)"),
                        [t[:, half, 0:1024] for t in (hi13, lo13)])
            return (raw13[:, slot, half, :, :].rearrange("p k n -> p (k n)"),
                    [t[:, half, :] for t in (hi13, lo13)])

        block = ctx.enter_context(nc.Block())

        @block.sync
        def _(sp):
            def free13(pair):
                if pair >= 2:
                    sp.wait_ge(lo13_done, 2 * (pair - 2) + 2)

            def load_pair(pair, srcs):
                free13(pair)
                for h in range(2):
                    dst = raw13[:, pair % 2, h, 0:srcs[h].shape[1], :]
                    sp.dma_start(dst, srcs[h]).then_inc(raw13_in[pair % 2], 16)

            def load_w2(f, q):
                n = NC * f + q
                if n >= 2:
                    sp.wait_ge(lo2_done, n - 1)
                sp.dma_start(raw2[:, n % 2, :], w2_v[f][:, q, :]).then_inc(raw2_in[n % 2], 16)

            def first_pair(unit, signal):
                for h in range(2):
                    c0 = unit * P
                    sp.dma_start(raw13[:, 0, h, :, c0:c0 + P], w13_v[0][:, :, h * DFF + c0:h * DFF + c0 + P]
                                 ).then_inc(signal, 16)

            sp.dma_start(cond[:, :], c_col).then_inc(cond_done, 16)
            sp.dma_start(ident[:, :], identity).then_inc(ident_in, 16)
            sp.dma_start(x[:, 0, :], x_v[:, 0, :]).then_inc(x_in_sem, 16)
            sp.dma_start(x[:, 1, :], x_v[:, 1, :]).then_inc(x_in_sem, 16)
            for m in range(6):
                g, j = (4 + 2 * m) // KT, (4 + 2 * m) % KT
                if m == 5:
                    first_pair(0, first_unit_in)
                sp.dma_start(first_ada[m], ada_v[0][:, j:j + 2, g * D:(g + 1) * D]).then_inc(first_in[m], 16)
            first_pair(1, raw13_in[0])
            for f in range(4):
                base = FFN_PAIR[f]
                for e in range(2):
                    if f == 0 and e == 0:
                        continue
                    if f == 0 and e == 1:
                        sp.wait_ge(ada_used, 2 * KT - 4)
                        load_w2(0, 0)
                    load_pair(base + e, [w13_v[f][:, :, h * DFF + e * 256:h * DFF + e * 256 + 256]
                                         for h in range(2)])
                    if f > 0 or e == 1:
                        load_w2(f, e)

                def turn(i):
                    for e in range(2):
                        pair = base + 2 + e
                        sp.wait_ge(lo13_done, 4 * i + (2 * pair - 2))
                        for h in range(2):
                            sp.dma_start(raw13[:, pair % 2, h, :, :],
                                         w13_v[f][:, :, bass.ds(i * 512 + (h * DFF + (2 + e) * 256), 256)]
                                         ).then_inc(raw13_in[pair % 2], 16)
                        for g in range(2):
                            load_w2_turn(i, 2 + 2 * e + g)

                def load_w2_turn(i, q):
                    n = NC * f + q
                    sp.wait_ge(lo2_done, 4 * i + (n - 1))
                    sp.dma_start(raw2[:, n % 2, :],
                                 w2_v[f][:, bass.ds(4 * i + q, 1), :].rearrange("p a n -> p (a n)")
                                 ).then_inc(raw2_in[n % 2], 16)

                with sp.Fori(0, 4) as i:
                    turn(i)
                load_pair(base + 10, [w13_v[f][:, :, h * DFF + 2560:h * DFF + 2816] for h in range(2)])
                for q in range(18, NC):
                    load_w2(f, q)
                if f == 0:
                    for t in range(TT):
                        for half in range(2):
                            rq = 2 * t + half
                            for rk in range(ROWS):
                                off = (rk - rq + NA_ROWS - 1) * (2 * NA_COLS - 1) + NA_COLS - GRID_W
                                src = bass.AP(tensor=b_rpb.tensor, offset=off,
                                              ap=[[1, GRID_W], [(2 * NA_ROWS - 1) * (2 * NA_COLS - 1), B_HEADS],
                                                  [1, GRID_W]])
                                sp.dma_start(bias[half * 64:half * 64 + 64, t, :, rk, :], src).then_inc(bias_in, 16)
                    for w in range(6):
                        c0 = 512 * WIN_COLS[w]
                        load_pair(WIN_PAIR + w, [win_v[:, :, c:c + 256] for c in (c0, c0 + 256)])
                    for w in range(2):
                        load_pair(WOUT_PAIR + w, [wout_v[:, :, w * 512 + h * 256:w * 512 + h * 256 + 256]
                                                  for h in range(2)])
                if f == 2:
                    load_pair(POOL_PAIR, [pw_v[:, 4 * h:4 * h + 4, :] for h in range(2)])
            sp.wait_ge(x_done, 2 * 5 + 1)
            sp.dma_start(out_v[:, 0, :], x[:, 0, :]).then_inc(out_sem, 16)
            sp.wait_ge(x_half, 4)
            sp.dma_start(out_v[:, 1, 0:512], x[:, 1, 0:512]).then_inc(out_sem, 16)
            sp.wait_ge(x_done, 2 * 5 + 2)
            sp.dma_start(out_v[:, 1, 512:D], x[:, 1, 512:D]).then_inc(out_sem, 16)
            sp.wait_ge(out_sem, 48)

        @block.gpsimd
        def _(pool):
            def ada_vector(g, first=0, last=KT):
                for j in range(first, last):
                    n = KT * g + j
                    if g > 0:
                        pool.wait_ge(ada_used, n - ADA_RING + 1)
                    pool.dma_start(ada[:, j % ADA_RING, :], ada_v[0][:, j, g * D:(g + 1) * D]
                                   ).then_inc(ada_in[j % ADA_RING], 16)

            ada_vector(0, 0, ADA_RING)
            nc.gpsimd.memset(neg_half[:, :], -0.5).then_inc(half_set, 1)

            def rms(width, wait_sem, wait_at, cols, tmp_at, plus):
                pool.wait_ge(wait_sem, wait_at)
                if width == 1:
                    nc.gpsimd.tensor_scalar(rstd[:, cols], ss[:, cols], plus, EPS, ALU.add, ALU.add
                                            ).then_inc(rstd_tmp, 1)
                else:
                    nc.gpsimd.tensor_scalar(rstd[:, cols], ss[:, cols], 1.0 / width, EPS, ALU.mult, ALU.add
                                            ).then_inc(rstd_tmp, 1)
                pool.wait_ge(rstd_tmp, tmp_at)
                nc.gpsimd.tensor_tensor(rstd[:, cols], rstd[:, cols], neg_half[:, cols], ALU.pow
                                        ).then_inc(rstd_done, 1)

            rms_n = [0]

            def next_rms(width, wait_sem, wait_at, cols, plus=0.0):
                rms_n[0] += 1
                rms(width, wait_sem, wait_at, cols, rms_n[0], plus)

            pool.wait_ge(half_set, 1)
            for t in range(TT):
                next_rms(1, ss_done, t + 1, slice(t, t + 1))

            def ada_loop(layer, m0, done, turns):
                with pool.Fori(0, turns) as i:
                    for j in range(KT):
                        pool.wait_ge(ada_used, KT * i + (KT * done + j - ADA_RING + 1))
                        pool.dma_start(ada[:, j % ADA_RING, :],
                                       ada_v[layer][:, j, bass.ds(i * D + m0 * D, D)]
                                       ).then_inc(ada_in[j % ADA_RING], 16)

            def norm_rms(s, halves=False):
                for t in range(TT):
                    next_rms(1, ss_done, 2 * s + t + 1, slice(t, t + 1),
                             plus=ss[:, 2:3] if halves and t == 1 else 0.0)

            ada_loop(0, 2, 2, 5)
            norm_rms(1, halves=True)
            ada_vector(7)
            def qk_rms(n):
                next_rms(HD, qred_done, n + 1, slice(16 * (n % 2), 16 * (n % 2) + 16))

            qk_rms(0)
            qk_rms(1)
            pool.wait_ge(bias_in, 16 * TT * 2 * ROWS)
            step = [0]
            for t in range(TT):
                for half in range(2):
                    rows = slice(half * 64, half * 64 + 64)
                    low = bias[rows, t, :, :, 0:48].rearrange("p h r c -> p (h r) c")
                    high = bias[rows, t, :, :, 16:64].rearrange("p h r c -> p (h r) c")
                    nc.gpsimd.affine_select(out=low, in_=low, compare_op=ALU.is_ge, fill=NEG,
                                            base=NA_COLS // 2 - (GRID_W - 1),
                                            pattern=[[0, 32], [1, 48]], channel_multiplier=1).then_inc(bias_done, 1)
                    step[0] += 1
                    pool.wait_ge(bias_done, step[0])
                    nc.gpsimd.affine_select(out=high, in_=high, compare_op=ALU.is_ge, fill=NEG,
                                            base=NA_COLS // 2 - 1 - NA_COLS + (GRID_W - 1),
                                            pattern=[[0, 32], [-1, 48]], channel_multiplier=-1).then_inc(bias_done, 1)
                    step[0] += 1
                    pool.wait_ge(bias_done, step[0])
            qk_rms(2)
            qk_rms(3)
            next_rms(P, ored_done, TT, slice(0, 8))
            norm_rms(2)
            ada_vector(8)
            ada_loop(1, 0, 9, 4)
            norm_rms(3, halves=True)
            ada_loop(1, 4, 13, 5)
            for n, src in enumerate((pool_b, pool_scale)):
                if n == 0:
                    pool.wait_ge(x_done, 2 * TT)
                pool.dma_start(v_sb[:, n, :], row_bcast(src, D)).then_inc(pool_in, 16)
            pool.dma_start(avg[:, :, :, :], pool_avg).then_inc(avg_in, 16)
            norm_rms(4, halves=True)
            norm_rms(5)

        @block.scalar
        def _(act):
            def split_hi(n, i=0):
                if n == 0:
                    act.wait_ge(first_unit_in, 32)
                else:
                    act.wait_ge(raw13_in[(n // 2) % 2], 32 * i + raw13_count(n // 2))
                if n >= 2:
                    act.wait_ge(unit_used, 4 * i + (n - 1))
                src, (hi, _) = unit_src(n)
                nc.scalar.activation(hi, src, ACT.Copy).then_inc(hi13_done, 1)

            def norm_squares(s, halves=0):
                for t in range(TT):
                    if t == 1 and halves:
                        for m in range(2):
                            if m == 0:
                                act.wait_ge(x_half, halves)
                            else:
                                act.wait_ge(x_done, 2 * s)
                            c = slice(m * D // 2, (m + 1) * D // 2)
                            ins = nc.scalar.activation(xn[:, 1, c], x[:, 1, c], ACT.Square, scale=D ** -0.5,
                                                       accum_out=ss[:, 1 + m:2 + m])
                        ins.then_inc(ss_done, 1)
                        continue
                    if s == 0:
                        act.wait_ge(x_in_sem, 32)
                    else:
                        act.wait_ge(x_done, 2 * (s - 1) + t + 1)
                    nc.scalar.activation(xn[:, t, :], x[:, t, :], ACT.Square, scale=D ** -0.5,
                                         accum_out=ss[:, t:t + 1]
                                         ).then_inc(ss_done, 1)

            def norm_out(s):
                g = NMOD * (s // 3) + 3 * (s % 3)
                act.wait_ge(acol_done, s + 1)
                for j in range(KT):
                    if j % 2 == 0:
                        act.wait_ge(xT_done, 4 * s + j // 2 + 1)
                    nc.scalar.activation(h32[:, j, :], ps[:, norm_bank(s, j), (j % 2) * 256:(j % 2) * 256 + 256],
                                         ACT.Identity, bias=modc[:, g, j:j + 1], scale=acol[:, s, j:j + 1]
                                         ).then_inc(h32_done, 1)

            def gate_copy(k, dst=gate[:, :]):
                act.wait_ge(gate_ps, k + 1)
                nc.scalar.activation(dst, ps[:, 6:8, :].rearrange("p b n -> p (b n)"), ACT.Copy
                                     ).then_inc(gate_ready, 1)

            def silu(Q, n, i4=0):
                act.wait_ge(unit_used, i4 + (n + 1))
                nc.scalar.activation(s_buf[:, Q % 2, :], ps[:, 4 + Q % 2, 0:256], ACT.Silu).then_inc(silu_done, 1)

            def u_high(Q, i4=0):
                act.wait_ge(u_done, i4 + (Q + 1))
                nc.scalar.activation(u_hi[:, Q % 2, :], u_buf[:, Q % 2, :], ACT.Copy).then_inc(uhi_done, 1)

            def w2_high(Q, i=0):
                act.wait_ge(raw2_in[Q % 2], 32 * i + 16 * (Q // 2 + 1))
                if Q >= 1:
                    act.wait_ge(w2_used, 4 * i + (Q + Q // NC))
                nc.scalar.activation(hi2[:, Q % 2, :], raw2[:, Q % 2, :], ACT.Copy).then_inc(hi2_done, 1)

            def ffn(f):
                Q0, n0 = NC * f, 2 * FFN_PAIR[f]
                split_hi(n0 + 1)
                w2_high(Q0)
                with act.Fori(0, 5) as i:
                    for q in range(1, 5):
                        silu(Q0 + q - 1, n0 + q - 1, 4 * i)
                        w2_high(Q0 + q, i)
                        u_high(Q0 + q - 1, 4 * i)
                        split_hi(n0 + q + 1, i)
                silu(Q0 + 20, n0 + 20)
                w2_high(Q0 + 21)
                u_high(Q0 + 20)
                silu(Q0 + 21, n0 + 21)
                u_high(Q0 + 21)
                gate_copy(SUB_OF_FFN[f])
                if f < 3:
                    split_hi(n0 + 22)

            act.dma_start(adab[:, :, :], ada_bT).then_inc(adab_in, 16)
            act.dma_start(exch[:, :], exchange).then_inc(small_in, 16)
            act.dma_start(ngT[:, :, :], norm_gT).then_inc(small_in, 16)
            act.dma_start(gnorm[:, :, :].rearrange("p a b -> p (a b)"), row_bcast(a_qk_norm, 2 * HD)
                          ).then_inc(small_in, 16)
            act.dma_start(bnorm[:, :], b_qk_normT).then_inc(small_in, 16)
            act.dma_start(rope[:, :, :, :], rope_cs).then_inc(small_in, 16)
            act.dma_start(subln[:, :], row_bcast(a_subln, P)).then_inc(small_in, 16)
            act.dma_start(lamb[:, :, :].rearrange("p a b -> p (a b)"), row_bcast(a_lambda, 4 * HD)
                          ).then_inc(small_in, 16)
            act.wait_ge(cond_done, 16)
            nc.scalar.activation(cond[:, :], cond[:, :], ACT.Silu).then_inc(cond_done, 1)
            norm_squares(0)
            split_hi(0)
            norm_out(0)
            ffn(0)
            norm_squares(1, halves=1)
            norm_out(1)

            def win_evac(w):
                n = 2 * WIN_PAIR + w
                act.wait_ge(unit_used, n + 1)
                seg, half = WIN_SEGS[w]
                if seg in ("va", "vb"):
                    c0 = (512 if seg == "vb" else 0) + half * 256
                    dst = v_sb[:, :, c0:c0 + 256]
                else:
                    c0 = (512 if seg[0] == "k" else 0) + half * 256
                    dst = xn[:, :, c0:c0 + 256]
                    if seg == "qb" and half == 0:
                        act.wait_ge(tp_fill, 4)
                if w == 0:
                    nc.scalar.activation(dst[:, 0, :], win_ps(0, 0), ACT.Copy)
                    nc.scalar.activation(dst[:, 1, :], win_ps(0, 1), ACT.Copy).then_inc(win_out, 1)
                else:
                    nc.scalar.activation(dst, ps[:, 4 + w % 2, :].rearrange("p (t n) -> p t n", t=TT), ACT.Copy
                                         ).then_inc(win_out, 1)

            tp = [0]

            def tp_evac(dst, scale=1.0):
                tp[0] += 1
                act.wait_ge(tp_fill, tp[0])
                nc.scalar.activation(dst, ps[:, (tp[0] - 1) % 2, :], ACT.Copy, scale=scale).then_inc(tp_out, 1)

            def qk_evac(ab, part):
                if ab == 1 and part == 0:
                    act.wait_ge(bnorm_done, 1)
                    act.wait_ge(score_done, 2 * A_HEADS)
                for b in (2 * part, 2 * part + 1):
                    tp_evac(qkT[:, 2 * b:2 * b + 2, :].rearrange("p b n -> p (b n)"),
                            1.0 if ab == 0 else bnorm[:, part:part + 1])

            def squares(n):
                act.wait_ge(win_out, (2, 4, 10, 12)[n])
                if n:
                    act.wait_ge(qred_done, n)
                c0 = (n % 2) * 512
                nc.scalar.activation(gate[:, :].rearrange("p (t n) -> p t n", t=TT), xn[:, :, c0:c0 + 512], ACT.Square
                                     ).then_inc(sq_done, 1)

            def exps(u):
                act.wait_ge(nmx_done, u + 1)
                if u >= 4:
                    act.wait_ge(tp_fill, slot_free(u))
                for t in range(TT):
                    nc.scalar.activation(e_buf[:, u % 4, t, :], ps[:, 6 + u % 2, t * 256:t * 256 + 256], ACT.Exp,
                                         bias=nmx[:, u, t:t + 1], accum_out=esum[:, u, t:t + 1]).then_inc(exp_done, 1)

            def weights_evac(k):
                if k >= 2:
                    act.wait_ge(pv_done, k - 1)
                tp_evac(ptT[k % 2][:, :, :].rearrange("p a n -> p (a n)"))

            n0 = 2 * WIN_PAIR
            for w in range(12):
                h = w - 9
                if w in (8, 9):
                    qk_evac(0, w - 8)
                if w >= 1:
                    win_evac(w - 1)
                if h >= 1:
                    weights_evac(h - 1)
                split_hi(n0 + w + 1)
                if w == 2:
                    act.wait_ge(lam_done, 1)
                    nc.scalar.activation(lam[:, 2:4], lam[:, 0:2], ACT.Exp).then_inc(lam_done, 1)
                if w == 3:
                    squares(0)
                if w == 4:
                    squares(1)
                if w == 10:
                    squares(2)
                if h >= 0:
                    exps(2 * h)
                    exps(2 * h + 1)
            win_evac(11)
            squares(3)
            weights_evac(2)
            exps(6)
            exps(7)
            qk_evac(1, 0)
            weights_evac(3)
            qk_evac(1, 1)
            act.wait_ge(pv_done, A_HEADS)
            for t in range(TT):
                nc.scalar.activation(mix[:, t, 0:512], ps[:, 2 + t, :], ACT.Square).then_inc(osq_done, 1)

            def b_output(m):
                act.wait_ge(pv_done, A_HEADS + 4 * m + 4)
                nc.scalar.activation(hT_hi[:, 4 + 2 * m:6 + 2 * m, :].rearrange("p j n -> p (j n)"), ps[:, 2 + m, :],
                                     ACT.Copy).then_inc(mixb_hi, 1)

            for b in range(B_HEADS + 2):
                if b < B_HEADS:
                    exps(8 + b)
                if b >= 2:
                    weights_evac(2 + b)
                if b == 3:
                    split_hi(n0 + 13)
                if b in (5, 6):
                    tp_evac(gate[:, (b - 5) * 512:(b - 5) * 512 + 512])
                if b == 8:
                    b_output(0)
            b_output(1)
            act.wait_ge(hlo_done, HLO[1] + 8 + 4)
            gate_copy(1)
            for n in (36, 37, 38):
                split_hi(n)
            norm_squares(2)
            norm_out(2)
            ffn(1)
            norm_squares(3, halves=2)
            norm_out(3)
            ffn(2)
            norm_squares(4, halves=3)
            gate_copy(4, pool_gate)
            split_hi(2 * POOL_PAIR + 1)
            norm_out(4)
            g4 = NMOD + 3
            for j in range(KT):
                act.wait_ge(pool_ps, j // 2 + 1)
                nc.scalar.activation(pooled[:, j, :], ps[:, POOL_BANK[j // 2], (j % 2) * 256:(j % 2) * 256 + 256],
                                     ACT.Identity, bias=modc[:, g4, j:j + 1], scale=acol[:, 4, j:j + 1]
                                     ).then_inc(pooled_done, 1)
            split_hi(2 * FFN_PAIR[3])
            norm_squares(5)
            norm_out(5)
            ffn(3)

        @block.vector
        def _(dve):
            V = nc.vector

            def split_lo(n, i4=0, part=None):
                dve.wait_ge(hi13_done, i4 + (n + 1))
                src, (hi, lo) = unit_src(n)
                if part is not None:
                    half = src.shape[1] // 2
                    src, hi, lo = (v[:, part * half:(part + 1) * half] for v in (src, hi, lo))
                ins = V.tensor_tensor(lo, src, hi.bitcast(F32), ALU.subtract)
                if part != 0:
                    ins.then_inc(lo13_done, 1)

            def w2_low(Q, i4=0):
                dve.wait_ge(hi2_done, i4 + (Q + 1))
                V.tensor_tensor(lo2[:, Q % 2, :], raw2[:, Q % 2, :], hi2[:, Q % 2, :].bitcast(F32), ALU.subtract
                                ).then_inc(lo2_done, 1)

            def u_mul(Q, i4=0, first=False):
                dve.wait_ge(silu_done, i4 + (Q + 1))
                V.tensor_tensor(u_buf[:, Q % 2, :], s_buf[:, Q % 2, :], b_ps(Q, first), ALU.mult
                                ).then_inc(u_done, 1)

            def u_low(Q, i4=0):
                dve.wait_ge(uhi_done, i4 + (Q + 1))
                V.tensor_tensor(u_lo[:, Q % 2, :], u_buf[:, Q % 2, :], u_hi[:, Q % 2, :].bitcast(F32), ALU.subtract
                                ).then_inc(ulo_done, 1)

            def ada_tile(g, j, i=0, gates=0):
                n = KT * g + j
                if ADA_RING <= n < 2 * KT:
                    m = (n - ADA_RING) // 2
                    dve.wait_ge(first_in[m], 16)
                    w = first_ada[m][:, n % 2, :]
                else:
                    uses = 1 if n < ADA_RING else n // ADA_RING - 2
                    dve.wait_ge(ada_in[j % ADA_RING], 32 * i + 16 * uses)
                    w = ada[:, j % ADA_RING, :]
                dst = acc_of(g)
                if j == 0:
                    if gates:
                        dve.wait_ge(gate_ps, gates)
                    if g == 1:
                        dve.wait_ge(xT_done, 4)
                    V.tensor_scalar(dst, w, cond[:, 0:1], None, ALU.mult).then_inc(ada_used, 1)
                else:
                    dve.wait_ge(ada_used, KT * i + (KT * g + j))
                    V.scalar_tensor_tensor(dst, w, cond[:, j:j + 1], dst, ALU.mult, ALU.add
                                           ).then_inc(ada_used, 1)

            def mod_out(g, i=0):
                dve.wait_ge(mod_ps, i + (g + 1))
                if isinstance(i, int):
                    dst, b = modc[:, g:g + 1, :], adab[:, g:g + 1, :]
                else:
                    dst, b = modc[:, bass.ds(i + g, 1), :], adab[:, bass.ds(i + g, 1), :]
                V.tensor_reduce(mraw[:, 0, :], ps[:, MOD_BANK:MOD_BANK + 2, :].rearrange("p b (k n) -> p (b k) n", n=P),
                                AX.X, ALU.add).then_inc(mod_red, 1)
                dve.wait_ge(mod_red, i + (g + 1))
                V.tensor_tensor(dst, mraw[:, :, :], b, ALU.add).then_inc(mod_done, 1)

            def diag(g, k, scale):
                dve.wait_ge(mod_done, g + 1)
                if k >= 1:
                    dve.wait_ge(gate_ps, k)
                for j in range(KT):
                    V.tensor_scalar(acc[:, j * P:(j + 1) * P], ident[:, :], modc[:, g, j:j + 1], scale,
                                    ALU.mult, ALU.mult).then_inc(diag_done, 1)

            def make_acol(s):
                g = NMOD * (s // 3) + 3 * (s % 3)
                dve.wait_ge(mod_done, g + 2)
                V.scalar_tensor_tensor(acol[:, s, :], modc[:, g + 1, :], 1.0, ngT[:, s, :], ALU.add, ALU.mult
                                       ).then_inc(acol_done, 1)

            def residual(s, sem_, at, halves=0):
                dve.wait_ge(gate_ready, s)
                for t in range(TT):
                    yb = MIX_Y_BANK[t] if s == 2 else 2 * t
                    parts = 2 if halves and t == 1 else 1
                    for m in range(parts):
                        if t == 0:
                            dve.wait_ge(y0_done, s)
                        elif m < parts - 1:
                            dve.wait_ge(y1_half, halves)
                        else:
                            dve.wait_ge(sem_, at)
                        c = slice(m * D // parts, (m + 1) * D // parts)
                        b0, b1 = yb + 2 * m // parts, yb + 2 * (m + 1) // parts
                        V.tensor_tensor(xn[:, t, c], ps[:, b0:b1, :].rearrange("p b n -> p (b n)"), gate[:, c], ALU.mult
                                        ).then_inc(x_tmp, 1)
                        xt_n[0] += 1
                        dve.wait_ge(x_tmp, xt_n[0])
                        V.tensor_tensor(x[:, t, c], x[:, t, c], xn[:, t, c], ALU.add
                                        ).then_inc(x_done if m == parts - 1 else x_half, 1)

            xt_n = [0]

            def norm_scale(s, tiles=range(TT)):
                for t in tiles:
                    dve.wait_ge(rstd_done, RS_AT[s] + t + 1)
                    V.tensor_scalar(xn[:, t, :], x[:, t, :], rstd[:, t:t + 1], None, ALU.mult).then_inc(xn_done, 1)

            def split_h(j, src=h32, n=2):
                h, hi, lo = (v[:, j:j + n, :].rearrange("p j n -> p (j n)") for v in (src, hT_hi, hT_lo))
                V.tensor_copy(hi, h).then_inc(hhi_done, 1)
                hhi_n[0] += 1
                dve.wait_ge(hhi_done, hhi_n[0])
                V.tensor_tensor(lo, h, hi.bitcast(F32), ALU.subtract).then_inc(hlo_done, n)

            hhi_n = [0]

            def norm_split(s):
                for j, n in ((0, 1), (1, 1), (2, 2), (4, 2), (6, 2)):
                    dve.wait_ge(h32_done, H32[s] + j + n)
                    split_h(j, n=n)

            def norm(s, n=None):
                norm_scale(s, [0])
                if n is not None:
                    split_lo(n, part=0)
                norm_scale(s, [1])
                if n is not None:
                    split_lo(n, part=1)
                norm_split(s)

            def ffn(f, m0=None, turns=0, gates=0):
                Q0, n0 = NC * f, 2 * FFN_PAIR[f]
                split_lo(n0 + 1)
                w2_low(Q0)

                def body(i, with_ada):
                    for d in range(4):
                        Q = Q0 + 1 + d
                        u_mul(Q - 1, 4 * i, first=isinstance(i, int) and i + d == 0)
                        if with_ada:
                            ada_tile(m0, 2 * d, i, gates)
                        u_low(Q - 1, 4 * i)
                        if with_ada:
                            ada_tile(m0, 2 * d + 1, i, gates)
                        w2_low(Q, 4 * i)
                        split_lo(n0 + d + 2, 4 * i)
                    if with_ada:
                        mod_out(m0, i)

                body(0, turns > 0)
                with dve.Fori(1, 5) as i:
                    body(i, turns > 0)
                u_mul(Q0 + 20)
                u_low(Q0 + 20)
                w2_low(Q0 + 21)
                diag(GATES[SUB_OF_FFN[f]], SUB_OF_FFN[f], 0.5)
                u_mul(Q0 + 21)
                u_low(Q0 + 21)

            V.memset(ones[:, :], 1.0).then_inc(setup_done, 1)
            norm_scale(0)
            dve.wait_ge(cond_done, 17)
            for g in range(2):
                for j in range(KT):
                    ada_tile(g, j)
                    if g == 1 and j == 3:
                        dve.wait_ge(adab_in, 16)
                        mod_out(0)
            split_lo(0)
            mod_out(1)
            dve.wait_ge(small_in, 16 * 7)
            make_acol(0)
            norm_split(0)
            ffn(0, m0=2, turns=5)
            V.tensor_scalar(bnorm[:, 0:1], bnorm[:, 0:1], SCALE, None, ALU.mult).then_inc(bnorm_done, 1)
            V.tensor_scalar(gnorm[:, 0, :], gnorm[:, 0, :], SCALE, None, ALU.mult).then_inc(setup_step, 1)
            dve.wait_ge(setup_step, 1)
            for cs in range(2):
                for t in range(TT):
                    V.tensor_tensor(rope_g[:, cs, t, :, :].rearrange("p q (h d) -> p (q h) d", d=32),
                                    gnorm[:, :, :].rearrange("p q (h d) -> p (q h) d", d=32),
                                    rope[:, cs, t, :].unsqueeze(1).to_broadcast([P, 4, 32]), ALU.mult
                                    ).then_inc(setup_step, 1)
            V.tensor_scalar(subln[:, :], subln[:, :], 1.0 - LAM0, None, ALU.mult).then_inc(setup_step, 1)
            V.tensor_tensor(lamb[:, 0:4:2, :], lamb[:, 0:4:2, :], lamb[:, 1:4:2, :], ALU.mult).then_inc(setup_step, 1)
            dve.wait_ge(setup_step, 7)
            V.tensor_reduce(lam[:, 0:2], lamb[:, 0:4:2, :], AX.X, ALU.add).then_inc(lam_done, 1)
            make_acol(1)
            residual(1, w2_used, w2_count(NC - 1), halves=1)
            norm(1, 22)

            def qk_sums(n):
                dve.wait_ge(sq_done, n + 1)
                V.tensor_reduce(ss[:, 16 * (n % 2):16 * (n % 2) + 16], gate[:, :].rearrange("p (g d) -> p g d", d=HD),
                                AX.X, ALU.add).then_inc(qred_done, 1)

            def qk_scale(n):
                dve.wait_ge(rstd_done, RS_AT[1] + 2 + n + 1)
                rs = rstd[:, 16 * (n % 2):16 * (n % 2) + 16].rearrange("p (t h) -> p t h", t=TT)
                for t in range(TT):
                    qk = xn[:, t, (n % 2) * 512:(n % 2) * 512 + 512].rearrange("p (h d) -> p h d", d=HD)
                    V.tensor_tensor(qk, qk, rs[:, t, :].unsqueeze(2).to_broadcast([P, 8, HD]), ALU.mult
                                    ).then_inc(qk_done if n >= 2 else qk_step, 1)

            def qk_tables(n, cs):
                dve.wait_ge(qk_step, 6 * n + 2)
                for t in range(TT):
                    qk = xn[:, t, n * 512:n * 512 + 512].rearrange("p (h d) -> p h d", d=HD)
                    V.tensor_tensor(mix[:, cs, t * 512:t * 512 + 512].rearrange("p (h d) -> p h d", d=HD), qk,
                                    rope_g[:, cs, t, n, :].unsqueeze(1).to_broadcast([P, 8, HD]), ALU.mult
                                    ).then_inc(qk_step, 1)

            def qk_rotate(n):
                dve.wait_ge(qk_step, 6 * n + 6)
                qk = xn[:, :, n * 512:n * 512 + 512].rearrange("p t (h d) -> p t h d", d=HD)
                xc, xs = (mix[:, cs, :].rearrange("p (t h d) -> p t h d", t=TT, d=HD) for cs in range(2))
                V.tensor_tensor(qk[:, :, :, 0:32], xc[:, :, :, 0:32], xs[:, :, :, 32:64], ALU.subtract
                                ).then_inc(qk_done, 1)
                V.tensor_tensor(qk[:, :, :, 32:64], xs[:, :, :, 0:32], xc[:, :, :, 32:64], ALU.add
                                ).then_inc(qk_done, 1)

            def row_max(u):
                dve.wait_ge(score_done, u + 1)
                V.tensor_reduce(nmx[:, u, :], ps[:, 6 + u % 2, :].rearrange("p (t n) -> p t n", t=TT), AX.X, ALU.max
                                ).then_inc(nmx_tmp, 1)
                dve.wait_ge(nmx_tmp, u + 1)
                V.tensor_scalar(nmx[:, u, :], nmx[:, u, :], -1.0, None, ALU.mult).then_inc(nmx_done, 1)

            def combine(h):
                dve.wait_ge(exp_done, 2 * (2 * h + 2))
                V.reciprocal(erec[:, 2 * h:2 * h + 2, :], esum[:, 2 * h:2 * h + 2, :]).then_inc(erec_done, 1)
                dve.wait_ge(erec_done, 2 * h + 1)
                V.tensor_scalar(erec[:, 2 * h + 1, :], erec[:, 2 * h + 1, :], lam[:, 0:1], None, ALU.mult
                                ).then_inc(erec_done, 1)
                dve.wait_ge(erec_done, 2 * h + 2)
                a, b = (2 * h) % 4, (2 * h + 1) % 4
                for t in range(TT):
                    V.tensor_scalar(e_buf[:, b, t, :], e_buf[:, b, t, :], erec[:, 2 * h + 1, t:t + 1], None, ALU.mult
                                    ).then_inc(comb_tmp, 1)
                for t in range(TT):
                    dve.wait_ge(comb_tmp, 2 * h + t + 1)
                    V.scalar_tensor_tensor(e_buf[:, a, t, :], e_buf[:, a, t, :], erec[:, 2 * h, t:t + 1],
                                           e_buf[:, b, t, :], ALU.mult, ALU.add).then_inc(comb_done, 1)

            n0 = 2 * WIN_PAIR
            for w in range(12):
                h = w - 9
                if h >= 0:
                    row_max(2 * h)
                    row_max(2 * h + 1)
                if w == 8:
                    qk_tables(1, 1)
                    qk_rotate(1)
                split_lo(n0 + w + 1)
                if w < 4:
                    for j in (2 * w, 2 * w + 1):
                        ada_tile(7, j, gates=1)
                if w == 3:
                    qk_sums(0)
                    dve.wait_ge(lam_done, 2)
                    V.tensor_tensor(lam[:, 0:1], lam[:, 3:4], lam[:, 2:3], ALU.subtract).then_inc(lam_done, 1)
                    dve.wait_ge(lam_done, 3)
                    V.tensor_scalar(lam[:, 0:1], lam[:, 0:1], -LAM0, None, ALU.add).then_inc(lam_done, 1)
                    dve.wait_ge(lam_done, 4)
                if w == 4:
                    qk_sums(1)
                    qk_scale(0)
                if w == 5:
                    mod_out(7)
                    qk_tables(0, 0)
                if w == 6:
                    qk_tables(0, 1)
                    qk_rotate(0)
                if w == 7:
                    qk_scale(1)
                    qk_tables(1, 0)
                if h >= 0:
                    combine(h)
                if w == 10:
                    qk_sums(2)
                if w == 11:
                    qk_scale(2)
            row_max(6)
            row_max(7)
            qk_sums(3)
            combine(3)
            qk_scale(3)
            diag(GATES[1], 1, 1.0)

            def a_output(t):
                dve.wait_ge(osq_done, t + 1)
                V.tensor_reduce(ss[:, 4 * t:4 * t + 4], mix[:, t, 0:512].rearrange("p (h d) -> p h d", d=P), AX.X,
                                ALU.add).then_inc(ored_done, 1)

            def a_scale(t):
                dve.wait_ge(rstd_done, RS_AT[1] + 2 + 4 + 1)
                m = mix[:, t, 0:512].rearrange("p (h d) -> p h d", d=P)
                V.tensor_tensor(m, ps[:, 2 + t, :].rearrange("p (h d) -> p h d", d=P),
                                rstd[:, 4 * t:4 * t + 4].unsqueeze(2).to_broadcast([P, 4, P]), ALU.mult
                                ).then_inc(omul_done, 1)
                dve.wait_ge(omul_done, t + 1)
                V.tensor_tensor(m, m, subln[:, :].unsqueeze(1).to_broadcast([P, 4, P]), ALU.mult
                                ).then_inc(mix_done, 1)

            def normalise(b):
                u = 2 * A_HEADS + b
                dve.wait_ge(exp_done, 2 * (u + 1))
                V.reciprocal(erec[:, u, :], esum[:, u, :]).then_inc(erec_done, 1)
                dve.wait_ge(erec_done, 2 * A_HEADS + b + 1)
                for t in range(TT):
                    V.tensor_scalar(e_buf[:, u % 4, t, :], e_buf[:, u % 4, t, :], erec[:, u, t:t + 1], None, ALU.mult
                                    ).then_inc(en_done, 1)

            def b_output(m):
                dve.wait_ge(mixb_hi, m + 1)
                hi, lo = (v[:, 4 + 2 * m:6 + 2 * m, :].rearrange("p j n -> p (j n)") for v in (hT_hi, hT_lo))
                V.tensor_tensor(lo, ps[:, 2 + m, :], hi.bitcast(F32), ALU.subtract).then_inc(hlo_done, 2)

            a_output(0)
            a_output(1)
            for b in range(B_HEADS + 1):
                if b < B_HEADS:
                    row_max(8 + b)
                if b >= 1:
                    normalise(b - 1)
                if b in (1, 2):
                    a_scale(b - 1)
                if b == 4:
                    split_lo(n0 + 13)
                if b in (7, 8):
                    dve.wait_ge(tp_out, TP_MIX[b - 7] + 1)
                    split_h(2 * (b - 7), gate[:, :].rearrange("p (j n) -> p j n", n=SEQ))
            b_output(0)
            b_output(1)
            for n in (36, 37):
                split_lo(n)
            make_acol(2)
            residual(2, unit_used, 2 * WOUT_PAIR + 4)
            norm(2, 2 * FFN_PAIR[1])
            ffn(1, m0=8, turns=5, gates=2)
            make_acol(3)
            residual(3, w2_used, w2_count(2 * NC - 1), halves=2)
            norm(3, 2 * FFN_PAIR[2])
            ffn(2, m0=13, turns=5, gates=3)
            make_acol(4)
            diag(GATES[4], 4, 1.0)
            residual(4, w2_used, w2_count(3 * NC - 1), halves=3)
            norm_scale(4, [0])
            split_lo(2 * POOL_PAIR)
            norm_scale(4, [1])

            split_lo(2 * POOL_PAIR + 1)
            dve.wait_ge(pool_in, 32)
            dve.wait_ge(gate_ready, 5)
            V.tensor_tensor(gate[:, :], pool_gate, v_sb[:, 1, :], ALU.mult).then_inc(pool_step, 1)
            for j2 in range(KT // 2):
                dve.wait_ge(h32_done, H32[4] + 2 * j2 + 2)
                dve.wait_ge(pooled_done, 2 * j2 + 2)
                d = pooled[:, 2 * j2:2 * j2 + 2, :]
                V.tensor_tensor(d, d, h32[:, 2 * j2:2 * j2 + 2, :], ALU.subtract).then_inc(diff_done, 1)
                dve.wait_ge(diff_done, j2 + 1)
                split_h(2 * j2, pooled)
            dve.wait_ge(pool_step, 1)
            make_acol(5)
            residual(5, unit_used, 2 * POOL_PAIR + 2)
            norm(5, 2 * FFN_PAIR[3])
            ffn(3)
            residual(6, w2_used, w2_count(4 * NC - 1), halves=4)

        @block.tensor
        def _(pe):
            mm = nc.tensor.matmul

            def norm(s):
                for t in range(TT):
                    pe.wait_ge(xn_done, 2 * s + t + 1)
                    for j in range(KT):
                        c0 = (j % 2) * 256 + t * P
                        ins = nc.tensor.transpose(ps[:, norm_bank(s, j), c0:c0 + P], xn[:, t, j * P:(j + 1) * P],
                                                  ident[:, :])
                        if t == TT - 1 and j % 2:
                            ins.then_inc(xT_done, 1)

            def three(out, pairs, first, last):
                for m, (a, b) in enumerate(pairs):
                    ins = mm(out, a, b, start=first and m == 0, stop=last and m == len(pairs) - 1)
                return ins

            def w13(s, Q, n, i4=0, hs=None):
                pe.wait_ge(lo13_done, i4 + (n + 1))
                order = ([(ab, k) for k in range(KT) for ab in range(2)] if hs is not None else
                         [(ab, k) for ab in range(2) for k in range(KT)])
                for ab, k in order:
                    if hs is not None and ab == 0:
                        pe.wait_ge(hlo_done, hs + k + 1)
                    w0 = (ab * KT + k) * P
                    wh, wl = hi13[:, n % 2, w0:w0 + P], lo13[:, n % 2, w0:w0 + P]
                    hh, hl = hT_hi[:, k, :], hT_lo[:, k, :]
                    dst = b_ps(Q, hs is not None) if ab else ps[:, 4 + Q % 2, 0:256]
                    ins = three(dst, ((wh, hh), (wh, hl), (wl, hh)), k == 0, k == KT - 1)
                    if hs is not None and (ab, k) == (0, KT - 1):
                        ins.then_inc(w2_used, 1)
                ins.then_inc(unit_used, 1)

            def w2_last(Q):
                p = Q % 2
                uh, ul = u_hi[:, p, P:2 * P], u_lo[:, p, P:2 * P]
                for h in range(2):
                    wh, wl = hi2[:, p, h * 512:h * 512 + 512], lo2[:, p, h * 512:h * 512 + 512]
                    for m, (a, b) in enumerate(((uh, wh), (uh, wl), (ul, wh))):
                        ins = mm(ps[:, 2 + h, :], a, b, start=False, stop=m == 2)
                    ins.then_inc(w2_used if h else y1_half, 1)

            def w2(Q, i4=0, tiles=range(TT), first=False, last=False, done=w2_used):
                pe.wait_ge(ulo_done, i4 + (Q + 1))
                pe.wait_ge(lo2_done, i4 + (Q + 1))
                p = Q % 2
                for t in tiles:
                    uh, ul = u_hi[:, p, t * P:(t + 1) * P], u_lo[:, p, t * P:(t + 1) * P]
                    for h in range(2):
                        wh, wl = hi2[:, p, h * 512:h * 512 + 512], lo2[:, p, h * 512:h * 512 + 512]
                        mm(ps[:, 2 * t + h, :], uh, wh, start=first, stop=False)
                        mm(ps[:, 2 * t + h, :], uh, wl, start=False, stop=False)
                    for h in range(2):
                        wh = hi2[:, p, h * 512:h * 512 + 512]
                        ins = mm(ps[:, 2 * t + h, :], ul, wh, start=False, stop=last)
                if done is not None:
                    ins.then_inc(done, 1)

            def mod_sum(g, i=0):
                pe.wait_ge(ada_used, KT * i + KT * (g + 1))
                if g >= 1:
                    pe.wait_ge(mod_done, i + g)
                for j in range(KT):
                    c0 = (j % 4) * P
                    ins = nc.tensor.transpose(ps[:, MOD_BANK + j // 4, c0:c0 + P], acc_of(g)[:, j * P:(j + 1) * P],
                                              ident[:, :])
                ins.then_inc(mod_ps, 1)

            def gate_row(k, mods):
                pe.wait_ge(diag_done, KT * (k + 1))
                pe.wait_ge(mod_done, mods)
                for h in range(2):
                    ins = mm(ps[:, 6 + h, :], ones[:, :], acc[:, h * 512:h * 512 + 512], start=True, stop=True)
                ins.then_inc(gate_ps, 1)

            def ffn(f, m0=None, turns=0, mods=0):
                s = SUB_OF_FFN[f]
                Q0, n0 = NC * f, 2 * FFN_PAIR[f]
                w13(s, Q0, n0, hs=HLO[s])

                def body(i, with_mod):
                    i4 = 4 * i
                    for d in range(4):
                        Q = Q0 + 1 + d
                        w13(s, Q, n0 + 1 + d, i4)
                        if with_mod and d == 3:
                            mod_sum(m0, i)
                        w2(Q - 1, i4, first=isinstance(i, int) and d == 0)

                body(0, turns > 0)
                with pe.Fori(1, 5) as i:
                    body(i, turns > 0)
                w13(s, Q0 + 21, n0 + 21)
                w2(Q0 + 20, tiles=[0], done=None)
                gate_row(s, mods)
                w2(Q0 + 21, tiles=[0], last=True, done=y0_done)
                w2(Q0 + 20, tiles=[1])
                w2_last(Q0 + 21)

            pe.wait_ge(setup_done, 1)
            pe.wait_ge(ident_in, 16)
            norm(0)
            mod_sum(0)
            mod_sum(1)
            ffn(0, m0=2, turns=5, mods=7)
            norm(1)

            def proj(n, hs=None, out_of=None, tiles=range(TT), ks=range(KT), done=None, y0=False, by_k=False):
                pe.wait_ge(lo13_done, n + 1)
                order = [(t, k) for k in ks for t in tiles] if by_k else [(t, k) for t in tiles for k in ks]
                for t, k in order:
                    if hs is not None and t == 0:
                        pe.wait_ge(hlo_done, hs + k + 1)
                    tok = slice(t * P, (t + 1) * P)
                    hh, hl = hT_hi[:, k, tok], hT_lo[:, k, tok]
                    wh, wl = hi13[:, n % 2, k * 256:k * 256 + 256], lo13[:, n % 2, k * 256:k * 256 + 256]
                    ins = three(out_of(t), ((hh, wh), (hh, wl), (hl, wh)), k == 0, k == KT - 1)
                    if y0 and (t, k) == (0, KT - 1):
                        ins.then_inc(y0_done, 1)
                if done or done is None and len(ks) == KT:
                    ins.then_inc(unit_used, 1)

            def wout_ps(v):
                return lambda t: ps[:, MIX_Y_BANK[t] + v // 2, (v % 2) * 256:(v % 2) * 256 + 256]

            tp = [0]

            def tp_bank():
                n = tp[0]
                if n >= 2:
                    pe.wait_ge(tp_out, n - 1)
                tp[0] += 1
                return n % 2

            def qk_transpose(ab, part):
                pe.wait_ge(qk_done, 4 * ab + 2 * part + 2)
                for b2 in (2 * part, 2 * part + 1):
                    bank = tp_bank()
                    for b in range(2):
                        for t in range(TT):
                            blk = 2 * b2 + b
                            ins = nc.tensor.transpose(ps[:, bank, b * 256 + t * P:b * 256 + t * P + P],
                                                      xn[:, t, blk * P:(blk + 1) * P], ident[:, :])
                    ins.then_inc(tp_fill, 1)

            def scores(u, tp_need):
                pe.wait_ge(tp_out, tp_need)
                if u >= 2:
                    pe.wait_ge(exp_done, 2 * (u - 1))
                v = u % (2 * A_HEADS)
                rows = slice((v % 2) * 64, (v % 2) * 64 + 64)
                for t in range(TT):
                    ins = mm(ps[:, 6 + u % 2, t * 256:t * 256 + 256], qkT[rows, v // 2, t * P:(t + 1) * P],
                             qkT[rows, 4 + v // 2, :], start=True, stop=u < 2 * A_HEADS)
                    if u >= 2 * A_HEADS:
                        ins = mm(ps[:, 6 + u % 2, t * 256:t * 256 + 256], exch[:, :],
                                 bias[:, t, v, :, :].rearrange("p r c -> p (r c)"), start=False, stop=True)
                ins.then_inc(score_done, 1)

            def weights_transpose(k):
                bank = tp_bank()
                if k < A_HEADS:
                    pe.wait_ge(comb_done, 2 * (k + 1))
                    slot = (2 * k) % 4
                else:
                    u = 2 * A_HEADS + k - A_HEADS
                    pe.wait_ge(en_done, 2 * (k - A_HEADS + 1))
                    slot = u % 4
                for kt in range(2):
                    for t in range(TT):
                        ins = nc.tensor.transpose(ps[:, bank, kt * 256 + t * P:kt * 256 + t * P + P],
                                                  e_buf[:, slot, t, kt * P:(kt + 1) * P], ident[:, :])
                ins.then_inc(tp_fill, 1)

            def values(k):
                pe.wait_ge(tp_out, tp_head(k) + 1)
                if k == 0:
                    pe.wait_ge(win_out, 6)
                if k == A_HEADS:
                    pe.wait_ge(win_out, 8)
                    pe.wait_ge(omul_done, 2)
                if k < A_HEADS:
                    for t in range(TT):
                        for kt in range(2):
                            ins = mm(ps[:, 2 + t, k * P:(k + 1) * P], ptT[k % 2][:, kt, t * P:(t + 1) * P],
                                     v_sb[:, kt, k * P:(k + 1) * P], start=kt == 0, stop=kt == 1)
                else:
                    b = k - A_HEADS
                    rows = slice((b % 2) * HD, (b % 2) * HD + HD)
                    dst = ps[rows, 2 + b // 4, (b // 2 % 2) * 256:(b // 2 % 2) * 256 + 256]
                    for kt in range(2):
                        ins = mm(dst, v_sb[:, kt, 512 + b * HD:512 + (b + 1) * HD], ptT[k % 2][:, kt, :],
                                 start=kt == 0, stop=kt == 1)
                ins.then_inc(pv_done, 1)

            n0 = 2 * WIN_PAIR
            for w in range(12):
                h = w - 9
                if w >= 2:
                    pe.wait_ge(win_out, w - 1)
                if h == 0:
                    pe.wait_ge(mod_done, 8)
                if h >= 0:
                    scores(2 * h, 4)
                    scores(2 * h + 1, 4)
                proj(n0 + w, hs=HLO[1] if w == 0 else None,
                     out_of=lambda t, w=w: win_ps(w, t), by_k=w == 0)
                if w == 4:
                    mod_sum(7)
                if w in (7, 8):
                    qk_transpose(0, w - 7)
                if h >= 0:
                    weights_transpose(h)
                if h >= 1:
                    values(h - 1)
            scores(6, 4)
            scores(7, 4)
            values(2)
            qk_transpose(1, 0)
            weights_transpose(3)
            values(3)
            qk_transpose(1, 1)
            pe.wait_ge(bias_done, 8)
            for b in range(B_HEADS + 3):
                if b < B_HEADS:
                    scores(8 + b, 12)
                if 2 <= b < B_HEADS + 2:
                    weights_transpose(2 + b)
                if b in (5, 6):
                    pe.wait_ge(mix_done, 2)
                    bank = tp_bank()
                    for jj in range(2):
                        for t in range(TT):
                            j = 2 * (b - 5) + jj
                            ins = nc.tensor.transpose(ps[:, bank, jj * 256 + t * P:jj * 256 + t * P + P],
                                                      mix[:, t, j * P:(j + 1) * P], ident[:, :])
                    ins.then_inc(tp_fill, 1)
                if b == 9:
                    pe.wait_ge(exp_done, 2 * (2 * A_HEADS + B_HEADS))
                    gate_row(1, 8)
                    proj(2 * WOUT_PAIR, hs=HLO[1] + 8, out_of=wout_ps(0), tiles=[0], ks=range(4))
                if b == 10:
                    pe.wait_ge(hlo_done, HLO[1] + 8 + 6)
                    proj(2 * WOUT_PAIR, out_of=wout_ps(0), tiles=[1], ks=range(4))
                if b >= 3:
                    values(1 + b)
            for t in range(TT):
                proj(2 * WOUT_PAIR, hs=HLO[1] + 8 if t == 0 else None, out_of=wout_ps(0), tiles=[t], ks=range(4, KT),
                     done=t == 1)
            for v in range(1, 4):
                proj(2 * WOUT_PAIR + v, out_of=wout_ps(v), y0=v == 3)
            norm(2)
            ffn(1, m0=8, turns=5, mods=13)
            norm(3)
            ffn(2, m0=13, turns=5, mods=18)
            pe.wait_ge(gate_ready, 4)
            gate_row(4, 18)
            norm(4)
            pe.wait_ge(avg_in, 16)
            for j in range(KT):
                if j == 4:
                    pe.wait_ge(gate_ready, 5)
                for kt in range(TT):
                    t0 = kt * (P - max(WINDOWS) // 2)
                    c0 = (j % 2) * 256
                    ins = mm(ps[:, POOL_BANK[j // 2], c0 + t0:c0 + SEQ], xn[:, kt, j * P:(j + 1) * P],
                             avg[:, j // 2, kt, t0:], start=kt == 0, stop=kt == 1)
                if j % 2:
                    ins.then_inc(pool_ps, 1)

            for g in range(4):
                n = 2 * POOL_PAIR + g // 2
                if g == 0:
                    pe.wait_ge(lo13_done, n + 2)
                    pe.wait_ge(pool_in, 32)
                    pe.wait_ge(pooled_done, 4)
                for t in range(TT):
                    mm(ps[:, 2 * t + g // 2, (g % 2) * 256:(g % 2) * 256 + 256], ident[:, :],
                       v_sb[:, 0, g * 256:(g + 1) * 256], start=True, stop=False)
                pe.wait_ge(hlo_done, HLO[4] + 2 * g + 2)
                for t in range(TT):
                    for kk in range(2):
                        k = 2 * g + kk
                        tok = slice(t * P, (t + 1) * P)
                        c0 = ((2 * g + kk) % 4) * 256
                        hh, hl = hT_hi[:, k, tok], hT_lo[:, k, tok]
                        wh, wl = hi13[:, n % 2, c0:c0 + 256], lo13[:, n % 2, c0:c0 + 256]
                        dst = ps[:, 2 * t + g // 2, (g % 2) * 256:(g % 2) * 256 + 256]
                        ins = three(dst, ((hh, wh), (hh, wl), (hl, wh)), False, kk == 1)
                    if g == 3 and t == 0:
                        ins.then_inc(y0_done, 1)
                if g % 2:
                    ins.then_inc(unit_used, 1)
            norm(5)
            ffn(3, mods=18)


def kernel(**inputs):
    import concourse.bacc as bacc
    from concourse.bass_utils import run_bass_kernel_spmd

    a = {k: np.ascontiguousarray(v) for k, v in inputs.items()}
    a["c"] = np.ascontiguousarray(a["c"].reshape(KT, P).T)
    a["ada_b"] = np.ascontiguousarray(a["ada_b"].reshape(2 * NMOD, KT, P).transpose(2, 0, 1))
    a["norm_g"] = np.ascontiguousarray(a["norm_g"].reshape(6, KT, P).transpose(2, 0, 1))
    a["b_qk_norm"] = np.ascontiguousarray(np.tile(a["b_qk_norm"][0].T, (2, 1)))
    inv = np.float32(10000.0) ** (-np.arange(0, HD, 2, dtype=np.float32) / np.float32(HD))
    ang = np.arange(SEQ, dtype=np.float32)[:, None] * inv[None, :]
    table = np.stack([np.cos(ang), np.sin(ang)]).astype(np.float32)
    a["rope_cs"] = np.ascontiguousarray(table.reshape(2, TT, P, HD // 2).transpose(2, 0, 1, 3))
    t = np.arange(SEQ)
    avg = []
    for w in WINDOWS:
        lo, hi = np.clip(t - w // 2, 0, SEQ), np.clip(t - w // 2 + w, 0, SEQ)
        avg.append(((t[:, None] >= lo) & (t[:, None] < hi)) / (hi - lo))
    avg = np.stack(avg, axis=1).astype(np.float32)
    a["pool_avg"] = np.ascontiguousarray(avg.reshape(TT, P, 4, SEQ).transpose(1, 2, 0, 3))
    a["identity"] = np.eye(P, dtype=np.float32)
    a["exchange"] = np.ascontiguousarray(a["identity"].reshape(P, 2, P // 2)[:, :, ::-1].reshape(P, P))

    nc = bacc.Bacc("TRN2", target_bir_lowering=False, num_devices=1)
    order = ["x", "c", "ada_w", "ada_b", "norm_g", "ff_w13", "ff_w2", "w_in", "w_out", "a_qk_norm",
             "a_lambda", "a_subln", "b_qk_norm", "b_rpb", "pool_w", "pool_b", "pool_scale",
             "rope_cs", "pool_avg", "identity", "exchange"]
    arrays, args = {}, []
    for name in order:
        arrays[f"in_{name}"] = a[name]
        args.append(nc.dram_tensor(f"in_{name}", a[name].shape, mybir.dt.from_np(a[name].dtype),
                                   kind="ExternalInput").ap())
    out = nc.dram_tensor("out_dram", (1, SEQ, D), F32, kind="ExternalOutput").ap()
    build_program(nc, *args, out)
    r = run_bass_kernel_spmd(nc, [arrays], core_ids=[0])
    return r.results[0]["out_dram"]
```
